# Optimizing a Trainium2 kernel written in Bass

```python
import jax, jax.numpy as jnp
from jax import lax
import numpy as np

D_MODEL = 1024
BATCH = 1
SEQ = 1024
DEPTH = 1
DEC_BATCH = 1
DEC_SEQ = 64
PAST_LEN = 512

CHUNK = 64
Q_BLOCK = 128
EPS = 1e-6
D_FF = 2816
SSD_HEADS = 8
SSD_HEAD_DIM = 64
SSD_WIDTH = SSD_HEADS * SSD_HEAD_DIM
SSD_GROUPS = 2
SSD_STATE = 128
SSD_CONV = 4
SSD_CONV_CH = SSD_WIDTH + 2 * SSD_GROUPS * SSD_STATE
GLA_HEADS = 4
GLA_DK = 32
GLA_DV = 64
GLA_WIDTH = GLA_HEADS * GLA_DV
GLA_RANK = 16
GLA_TAU = 16.0
FOX_HEADS = 4
FOX_HEAD_DIM = 64
FOX_WIDTH = FOX_HEADS * FOX_HEAD_DIM
D_MIX = SSD_WIDTH + GLA_WIDTH + FOX_WIDTH
IN_SPLITS = (SSD_WIDTH, SSD_CONV_CH, SSD_HEADS,
             GLA_HEADS * GLA_DK, GLA_HEADS * GLA_DK, GLA_WIDTH, GLA_WIDTH, GLA_RANK,
             FOX_WIDTH, FOX_WIDTH, FOX_WIDTH, FOX_HEADS)
IN_COLS = sum(IN_SPLITS)

kernel_name = 'hybrid_ssd_gla_fox_macaron_step'

def split_cols(a, sizes):
    out, off = [], 0
    for s in sizes:
        out.append(a[..., off:off + s])
        off += s
    return out

def rmsnorm(x, w):
    xf = x.astype(jnp.float32)
    y = xf * lax.rsqrt(jnp.mean(xf * xf, axis=-1, keepdims=True) + EPS)
    return (y * w.astype(jnp.float32)).astype(x.dtype)

def swiglu(h, w_gate, w_up, w_down):
    return (jax.nn.silu(h @ w_gate) * (h @ w_up)) @ w_down

def causal_conv(u, prev, w, b):
    T = u.shape[1]
    up = jnp.concatenate([prev.astype(u.dtype), u], axis=1)
    y = up[:, 0:T] * w[0]
    for j in range(1, SSD_CONV):
        y = y + up[:, j:j + T] * w[j]
    return jax.nn.silu(y + b), up[:, -(SSD_CONV - 1):]

def ssd_scan(x, dt, A, Bm, Cm, h0):
    Bsz, T, H, P = x.shape
    G, N = Bm.shape[2], Bm.shape[3]
    L = min(CHUNK, T)
    nc = T // L
    x = x.reshape(Bsz, nc, L, H, P)
    dt = dt.reshape(Bsz, nc, L, H)
    Bm = Bm.reshape(Bsz, nc, L, G, N)
    Cm = Cm.reshape(Bsz, nc, L, G, N)
    hg = jnp.arange(H) // (H // G)
    acum = jnp.cumsum(dt * A, axis=2)
    cb = jnp.einsum('bclgn,bcsgn->bclsg', Cm, Bm)[..., hg]
    causal = jnp.tril(jnp.ones((L, L), dtype=bool))[None, None, :, :, None]
    seg = acum[:, :, :, None, :] - acum[:, :, None, :, :]
    decay = jnp.where(causal, jnp.exp(jnp.where(causal, seg, 0.0)), 0.0)
    y_intra = jnp.einsum('bclsh,bcsh,bcshp->bclhp', cb * decay, dt, x)
    Bh = Bm[..., hg, :]
    Ch = Cm[..., hg, :]
    decay_end = jnp.exp(acum[:, :, -1:, :] - acum)
    states = jnp.einsum('bclh,bclhn,bclhp->bchpn', decay_end * dt, Bh, x)
    chunk_decay = jnp.exp(acum[:, :, -1, :])

    def step(h, inp):
        st, cd = inp
        return h * cd[:, :, None, None] + st, h

    h_last, h_prev = lax.scan(step, h0, (jnp.moveaxis(states, 1, 0), jnp.moveaxis(chunk_decay, 1, 0)))
    h_prev = jnp.moveaxis(h_prev, 0, 1)
    y_inter = jnp.einsum('bclhn,bchpn,bclh->bclhp', Ch, h_prev, jnp.exp(acum))
    return (y_intra + y_inter).reshape(Bsz, T, H, P), h_last

def gla_scan(q, k, v, la, s0):
    Bsz, T, H, K = q.shape
    V = v.shape[-1]
    L = min(CHUNK, T)
    nc = T // L
    q = q.reshape(Bsz, nc, L, H, K)
    k = k.reshape(Bsz, nc, L, H, K)
    v = v.reshape(Bsz, nc, L, H, V)
    bcum = jnp.cumsum(la.reshape(Bsz, nc, L, H, K), axis=2)
    qd = q * jnp.exp(bcum)
    kd = k * jnp.exp(-bcum)
    causal = jnp.tril(jnp.ones((L, L), dtype=bool))
    att = jnp.where(causal, jnp.einsum('bclhk,bcshk->bchls', qd, kd), 0.0)
    o_intra = jnp.einsum('bchls,bcshv->bclhv', att, v)
    blast = bcum[:, :, -1]
    kend = k * jnp.exp(blast[:, :, None] - bcum)
    states = jnp.einsum('bclhk,bclhv->bchkv', kend, v)

    def step(S, inp):
        st, bl = inp
        return S * jnp.exp(bl)[..., None] + st, S

    s_last, s_prev = lax.scan(step, s0, (jnp.moveaxis(states, 1, 0), jnp.moveaxis(blast, 1, 0)))
    s_prev = jnp.moveaxis(s_prev, 0, 1)
    o_inter = jnp.einsum('bclhk,bchkv->bclhv', qd, s_prev)
    return (o_intra + o_inter).reshape(Bsz, T, H, V), s_last

def fox_attend(q, k, v, cq, ck, qpos, kpos):
    f32 = jnp.float32
    s = jnp.einsum('bqhd,bkhd->bhqk', q.astype(f32), k.astype(f32)) * (FOX_HEAD_DIM ** -0.5)
    s = s + (jnp.swapaxes(cq, 1, 2)[..., :, None] - jnp.swapaxes(ck, 1, 2)[..., None, :])
    s = jnp.where(kpos[None, :] <= qpos[:, None], s, -jnp.inf)
    p = jax.nn.softmax(s, axis=-1)
    return jnp.einsum('bhqk,bkhd->bqhd', p, v.astype(f32))

def fox_prompt(q, k, v, c):
    B, T, H, D = q.shape
    nb = T // Q_BLOCK
    kpos = jnp.arange(T)
    qb = jnp.swapaxes(q.reshape(B, nb, Q_BLOCK, H, D), 0, 1)
    cb = jnp.swapaxes(c.reshape(B, nb, Q_BLOCK, H), 0, 1)

    def blk(args):
        i, qi, ci = args
        qpos = i * Q_BLOCK + jnp.arange(Q_BLOCK)
        return fox_attend(qi, k, v, ci, c, qpos, kpos)

    o = lax.map(blk, (jnp.arange(nb), qb, cb))
    return jnp.swapaxes(o, 0, 1).reshape(B, T, H, D)

def token_mix(h, p, past):
    conv_prev, ssd_h0, gla_s0, k_past, v_past, lf_past = past
    B, T, _ = h.shape
    f32 = jnp.float32
    u = h @ p['w_in']
    (z, xbc, dt_raw, gq, gk, gv, gg, gr, fq, fk, fv, ff) = split_cols(u, IN_SPLITS)

    xbc_act, conv_new = causal_conv(xbc, conv_prev, p['ssd_conv_w'], p['ssd_conv_b'])
    xs, bs, cs = split_cols(xbc_act.astype(f32), (SSD_WIDTH, SSD_GROUPS * SSD_STATE, SSD_GROUPS * SSD_STATE))
    xs = xs.reshape(B, T, SSD_HEADS, SSD_HEAD_DIM)
    bs = bs.reshape(B, T, SSD_GROUPS, SSD_STATE)
    cs = cs.reshape(B, T, SSD_GROUPS, SSD_STATE)
    dt = jax.nn.softplus(dt_raw.astype(f32) + p['ssd_dt_bias'].astype(f32))
    A = -jnp.exp(p['ssd_a_log'].astype(f32))
    y_ssd, ssd_new = ssd_scan(xs, dt, A, bs, cs, ssd_h0.astype(f32))
    y_ssd = y_ssd + p['ssd_d'].astype(f32)[:, None] * xs
    y_ssd = y_ssd.reshape(B, T, SSD_WIDTH) * jax.nn.silu(z.astype(f32))
    y_ssd = rmsnorm(y_ssd.reshape(B, T, SSD_GROUPS, SSD_WIDTH // SSD_GROUPS),
                    p['ssd_norm'].reshape(SSD_GROUPS, SSD_WIDTH // SSD_GROUPS)).reshape(B, T, SSD_WIDTH)

    q = gq.astype(f32).reshape(B, T, GLA_HEADS, GLA_DK) * (GLA_DK ** -0.5)
    k = gk.astype(f32).reshape(B, T, GLA_HEADS, GLA_DK)
    v = gv.astype(f32).reshape(B, T, GLA_HEADS, GLA_DV)
    la = jax.nn.log_sigmoid((gr @ p['gla_w_gate'] + p['gla_b_gate']).astype(f32)) / GLA_TAU
    o_gla, gla_new = gla_scan(q, k, v, la.reshape(B, T, GLA_HEADS, GLA_DK), gla_s0.astype(f32))
    o_gla = rmsnorm(o_gla, p['gla_norm']) * jax.nn.silu(gg.astype(f32).reshape(B, T, GLA_HEADS, GLA_DV))
    o_gla = o_gla.reshape(B, T, GLA_WIDTH)

    fq_n = rmsnorm(fq.reshape(B, T, FOX_HEADS, FOX_HEAD_DIM), p['fox_q_norm'])
    fk_n = rmsnorm(fk.reshape(B, T, FOX_HEADS, FOX_HEAD_DIM), p['fox_k_norm'])
    fv_h = fv.reshape(B, T, FOX_HEADS, FOX_HEAD_DIM)
    lf = jax.nn.log_sigmoid(ff.astype(f32) + p['fox_f_bias'].astype(f32))
    if k_past is None:
        o_fox = fox_prompt(fq_n, fk_n, fv_h, jnp.cumsum(lf, axis=1))
    else:
        P = k_past.shape[1]
        k_all = jnp.concatenate([k_past.astype(fk_n.dtype), fk_n], axis=1)
        v_all = jnp.concatenate([v_past.astype(fv_h.dtype), fv_h], axis=1)
        c_all = jnp.cumsum(jnp.concatenate([lf_past.astype(f32), lf], axis=1), axis=1)
        o_fox = fox_attend(fq_n, k_all, v_all, c_all[:, P:], c_all, P + jnp.arange(T), jnp.arange(P + T))
    o_fox = o_fox.reshape(B, T, FOX_WIDTH)

    mixed = jnp.concatenate([y_ssd.astype(f32), o_gla, o_fox], axis=-1).astype(h.dtype)
    out = mixed @ p['w_out']
    dt_out = h.dtype
    new_state = (conv_new.astype(dt_out), ssd_new.astype(dt_out), gla_new.astype(dt_out),
                 fk_n.astype(dt_out), fv_h.astype(dt_out), lf.astype(dt_out))
    return out, new_state

def trunk_layer(x, p, past):
    x = x + (0.5 * swiglu(rmsnorm(x, p['norm_ffn1']), p['w1_gate'], p['w1_up'], p['w1_down'])).astype(x.dtype)
    y, new_state = token_mix(rmsnorm(x, p['norm_mix']), p, past)
    x = x + y.astype(x.dtype)
    x = x + (0.5 * swiglu(rmsnorm(x, p['norm_ffn2']), p['w2_gate'], p['w2_up'], p['w2_down'])).astype(x.dtype)
    return x, new_state

def setup_inputs(seed: int = 0) -> dict:
    key = jax.random.key(seed)
    ks = iter(jax.random.split(key, 48))
    f32 = jnp.float32

    def nrm(shape, scale=1.0):
        return scale * jax.random.normal(next(ks), shape, f32)

    def gain(shape):
        return 1.0 + 0.1 * jax.random.normal(next(ks), shape, f32)

    dt0 = jnp.exp(jax.random.uniform(next(ks), (DEPTH, SSD_HEADS), f32, np.log(1e-3), np.log(1e-1)))
    d = {}
    d['x_prompt'] = nrm((BATCH, SEQ, D_MODEL))
    d['x_sample'] = nrm((DEC_BATCH, DEC_SEQ, D_MODEL))
    d['state_ssd_conv'] = nrm((DEPTH, DEC_BATCH, SSD_CONV - 1, SSD_CONV_CH))
    d['state_ssd'] = nrm((DEPTH, DEC_BATCH, SSD_HEADS, SSD_HEAD_DIM, SSD_STATE), 0.3)
    d['state_gla'] = nrm((DEPTH, DEC_BATCH, GLA_HEADS, GLA_DK, GLA_DV), 0.3)
    d['cache_fox_k'] = nrm((DEPTH, DEC_BATCH, PAST_LEN, FOX_HEADS, FOX_HEAD_DIM))
    d['cache_fox_v'] = nrm((DEPTH, DEC_BATCH, PAST_LEN, FOX_HEADS, FOX_HEAD_DIM))
    d['cache_fox_logf'] = jax.nn.log_sigmoid(2.0 + nrm((DEPTH, DEC_BATCH, PAST_LEN, FOX_HEADS)))
    d['norm_ffn1'] = gain((DEPTH, D_MODEL))
    d['w1_gate'] = nrm((DEPTH, D_MODEL, D_FF), D_MODEL ** -0.5)
    d['w1_up'] = nrm((DEPTH, D_MODEL, D_FF), D_MODEL ** -0.5)
    d['w1_down'] = nrm((DEPTH, D_FF, D_MODEL), D_FF ** -0.5)
    d['norm_mix'] = gain((DEPTH, D_MODEL))
    d['w_in'] = nrm((DEPTH, D_MODEL, IN_COLS), D_MODEL ** -0.5)
    d['ssd_conv_w'] = nrm((DEPTH, SSD_CONV, SSD_CONV_CH), SSD_CONV ** -0.5)
    d['ssd_conv_b'] = nrm((DEPTH, SSD_CONV_CH), 0.05)
    d['ssd_dt_bias'] = dt0 + jnp.log(-jnp.expm1(-dt0))
    d['ssd_a_log'] = jnp.log(jax.random.uniform(next(ks), (DEPTH, SSD_HEADS), f32, 1.0, 16.0))
    d['ssd_d'] = gain((DEPTH, SSD_HEADS))
    d['ssd_norm'] = gain((DEPTH, SSD_WIDTH))
    d['gla_w_gate'] = nrm((DEPTH, GLA_RANK, GLA_HEADS * GLA_DK), GLA_RANK ** -0.5)
    d['gla_b_gate'] = nrm((DEPTH, GLA_HEADS * GLA_DK), 0.05)
    d['gla_norm'] = gain((DEPTH, GLA_DV))
    d['fox_q_norm'] = gain((DEPTH, FOX_HEAD_DIM))
    d['fox_k_norm'] = gain((DEPTH, FOX_HEAD_DIM))
    d['fox_f_bias'] = 2.0 + nrm((DEPTH, FOX_HEADS), 0.5)
    d['w_out'] = nrm((DEPTH, D_MIX, D_MODEL), D_MIX ** -0.5)
    d['norm_ffn2'] = gain((DEPTH, D_MODEL))
    d['w2_gate'] = nrm((DEPTH, D_MODEL, D_FF), D_MODEL ** -0.5)
    d['w2_up'] = nrm((DEPTH, D_MODEL, D_FF), D_MODEL ** -0.5)
    d['w2_down'] = nrm((DEPTH, D_FF, D_MODEL), D_FF ** -0.5)
    return d

def reference(x_prompt, x_sample, state_ssd_conv, state_ssd, state_gla, cache_fox_k, cache_fox_v,
              cache_fox_logf, norm_ffn1, w1_gate, w1_up, w1_down, norm_mix, w_in, ssd_conv_w,
              ssd_conv_b, ssd_dt_bias, ssd_a_log, ssd_d, ssd_norm, gla_w_gate, gla_b_gate, gla_norm,
              fox_q_norm, fox_k_norm, fox_f_bias, w_out, norm_ffn2, w2_gate, w2_up, w2_down):
    xp, xs = x_prompt, x_sample
    bp = xp.shape[0]
    p_new = [[] for _ in range(6)]
    s_new = [[] for _ in range(6)]
    for l in range(DEPTH):
        prm = dict(norm_ffn1=norm_ffn1[l], w1_gate=w1_gate[l], w1_up=w1_up[l], w1_down=w1_down[l],
                   norm_mix=norm_mix[l], w_in=w_in[l], ssd_conv_w=ssd_conv_w[l], ssd_conv_b=ssd_conv_b[l],
                   ssd_dt_bias=ssd_dt_bias[l], ssd_a_log=ssd_a_log[l], ssd_d=ssd_d[l], ssd_norm=ssd_norm[l],
                   gla_w_gate=gla_w_gate[l], gla_b_gate=gla_b_gate[l], gla_norm=gla_norm[l],
                   fox_q_norm=fox_q_norm[l], fox_k_norm=fox_k_norm[l], fox_f_bias=fox_f_bias[l],
                   w_out=w_out[l], norm_ffn2=norm_ffn2[l], w2_gate=w2_gate[l], w2_up=w2_up[l],
                   w2_down=w2_down[l])
        prompt_past = (jnp.zeros((bp, SSD_CONV - 1, SSD_CONV_CH), xp.dtype),
                       jnp.zeros((bp, SSD_HEADS, SSD_HEAD_DIM, SSD_STATE), jnp.float32),
                       jnp.zeros((bp, GLA_HEADS, GLA_DK, GLA_DV), jnp.float32),
                       None, None, None)
        sample_past = (state_ssd_conv[l], state_ssd[l], state_gla[l],
                       cache_fox_k[l], cache_fox_v[l], cache_fox_logf[l])
        xp, st_p = trunk_layer(xp, prm, prompt_past)
        xs, st_s = trunk_layer(xs, prm, sample_past)
        for i in range(6):
            p_new[i].append(st_p[i])
            s_new[i].append(st_s[i])
    p_ssd_conv, p_ssd, p_gla, p_fox_k, p_fox_v, p_fox_logf = [jnp.stack(a) for a in p_new]
    s_ssd_conv, s_ssd, s_gla, s_fox_k, s_fox_v, s_fox_logf = [jnp.stack(a) for a in s_new]
    return (xp, xs, p_ssd_conv, p_ssd, p_gla, p_fox_k, p_fox_v, p_fox_logf,
            s_ssd_conv, s_ssd, s_gla, s_fox_k, s_fox_v, s_fox_logf)


_drawn_inputs = setup_inputs


def setup_inputs(seed=0):
    import zlib

    import numpy as np

    out = dict(_drawn_inputs(seed))
    spreads = {}
    factors = {'state_gla': 2.76,
     'cache_fox_logf': 8.0,
     'gla_b_gate': 2.703,
     'gla_norm': 2.902,
     'fox_q_norm': 4.586}
    for name, (base, spread) in spreads.items():
        noise = np.random.default_rng([zlib.crc32(name.encode()), seed]).standard_normal(out[name].shape)
        drawn = base * np.exp(spread * noise) if base else spread * noise
        out[name] = __import__('jax').numpy.asarray(drawn.astype(out[name].dtype))
    for name, factor in factors.items():
        out[name] = (out[name] * factor).astype(out[name].dtype)
    return out
```

```python
from contextlib import ExitStack

import numpy as np

import concourse.bass as bass
from concourse import mybir

ALU = mybir.AluOpType
ACT = mybir.ActivationFunctionType
F32 = mybir.dt.float32
F32R = mybir.dt.float32r
I32 = mybir.dt.int32

P = 128
D = 1024
KT = D // P
TP, TS = 1024, 64
T = TP + TS
PIECES = ((0, 364), (364, 726), (726, T))
NPC = len(PIECES)
W = 364
FF = 2816
FT = FF // P
PAST = 512
EPS = 1e-6
BIG = 1e30
LOG_EXP = "natural_log_exp_and_others"

SSD_H, SSD_P, SSD_N = 8, 64, 128
GLA_H, GLA_K, GLA_V, GLA_R, GLA_TAU = 4, 32, 64, 16, 16.0
FOX_H, FOX_D = 4, 64
TILES = [(j * P, min(P, T - j * P)) for j in range((T + P - 1) // P)]
NTT = len(TILES)
SMALL_DT, SMALL_FF = 32, 64

STEP = 2 * D
FFN_STEPS = FT + FT // 2
IN_STEPS = 13
OUT_STEPS = 4
BASE1 = 0
BASE_IN = FFN_STEPS
BASE_OUT = BASE_IN + IN_STEPS
BASE2 = BASE_OUT + OUT_STEPS
NSTEPS = BASE2 + FFN_STEPS

IN_PLAN = [("fq0", "fq1"), ("fk0", "fk1"), ("small", "gk"), "fv", ("gq",), "gv", ("gg0", "gg1"),
           ("x0", "x1"), ("x2", "x3"), ("x4", "x5"), ("x6", "x7"), ("z0", "z1"), ("z2", "z3")]
IN_PIECES = [NTT if isinstance(s, str) else NPC * len(s) for s in IN_PLAN]
IN_START = [sum(IN_PIECES[:t]) for t in range(IN_STEPS + 1)]
FOX_AT, GLA_AT, CONV_AT = 4, 7, 7

C_ID, C_ONE, C_B64, C_MQK, C_MSL, C_GM, C_BM, C_SEL = 0, 128, 256, 384, 512, 640, 768, 1024
NCONST = C_SEL + SSD_H * P
V_N1, V_NM, V_N2, V_CW, V_CB, V_SB, V_AL, V_D, V_SN, V_GB, V_GN, V_QN, V_KN = (
    0, 8, 16, 24, 56, 64, 65, 66, 70, 74, 75, 76, 77)
NVEC = 78
CUM = TP + PAST + TS


def at(i, per_body, c):
    return c if i is None else i * per_body + c


def wait(e, sem, value):
    if not isinstance(value, int) or value > 0:
        e.wait_ge(sem, value)


class Chain:

    def __init__(self, e, sem):
        self.e, self.sem, self.n = e, sem, 0

    def __call__(self, ins):
        self.n += 1
        ins.then_inc(self.sem, 1)
        self.e.wait_ge(self.sem, self.n)


def split_hi(K, e, S, parity):
    e.wait_ge(K.w_loaded, 16 * (S + 1))
    K.nc.scalar.copy(K.whi[:, parity], K.wraw[:]).then_inc(K.w_hi, 1)


def split_lo(K, e, S, parity, halves=(0, 1)):
    for h in halves:
        c = slice(h * D, h * D + D)
        if h == 0:
            e.wait_ge(K.w_hi, S + 1)
        K.nc.vector.tensor_tensor(K.wlo[:, parity, c], K.wraw[:, c], K.whi[:, parity, c].bitcast(F32),
                                  ALU.subtract).then_inc(K.w_lo, 1)


def three(K, out, whi, wlo, xhi, xlo, first, last, token_major=False, skip=False):
    mm = None
    for n, (w, x) in enumerate(((whi, xhi), (whi, xlo), (wlo, xhi))):
        a, b = (x, w) if token_major else (w, x)
        mm = K.nc.tensor.matmul(out, a, b, start=first and n == 0, stop=last and n == 2)
    return mm


SUMS_FIRST, SUMS_LATER = KT, 1


def follow_act(K, e, N, updated, base, tiles=range(KT)):
    for d in tiles:
        for j, (a, b) in enumerate(PIECES):
            o = NPC * d + j
            e.wait_ge(updated, base + o + 1)
            wait(e, N.added, o - 2 * NPC)
            dst = K.rms[:, a:b] if d == 0 else K.sqs[:, (o - NPC) % 4, :b - a]
            K.nc.scalar.activation(dst, K.x[:, d, a:b], ACT.Square).then_inc(N.sq, 1)


def follow_pool(K, e, N):
    for d in range(1, KT):
        for j, (a, b) in enumerate(PIECES):
            o = NPC * d + j
            e.wait_ge(N.sq, o + 1)
            wait(e, N.added, o - 2 * NPC + 1)
            K.nc.gpsimd.tensor_tensor(K.rms[:, a:b], K.rms[:, a:b], K.sqs[:, (o - NPC) % 4, :b - a],
                                      ALU.add).then_inc(N.added, 1)


def follow_pe(K, e, N):
    for c, (a, b) in enumerate(PIECES):
        e.wait_ge(N.added, NPC * (KT - 2) + c + 1)
        K.nc.tensor.matmul(K.ps[:, 4 + c, :b - a], K.ones, K.rms[:, a:b], start=True,
                           stop=True).then_inc(N.sum_mm, 1)


def first_sums_pe(K, e, N):
    for c, (a, b) in enumerate(PIECES):
        for k in range(KT):
            n = KT * c + k
            e.wait_ge(N.sq, n + 1)
            K.nc.tensor.matmul(K.ps[:, 4 + c, :b - a], K.ones, K.sq_first[:, n % 4, :b - a],
                               start=k == 0, stop=k == KT - 1).then_inc(N.sum_mm, 1)


def norm_act(K, e, N, sums):
    nc = K.nc

    def square(c, k):
        a, b = PIECES[c]
        n = KT * c + k
        if k == 0:
            e.wait_ge(K.x_in[c], 16)
        wait(e, N.sum_mm, n - 3)
        nc.scalar.activation(K.sq_first[:, n % 4, :b - a], K.x[:, k, a:b], ACT.Square).then_inc(N.sq, 1)

    def rms(c):
        a, b = PIECES[c]
        e.wait_ge(N.sum_mm, sums * (c + 1))
        K.act(nc.scalar.activation(K.rms[:, a:b], K.ps[:, 4 + c, :b - a], ACT.Ln, bias=K.eps[:, 0:1],
                                   scale=1.0 / D))
        nc.scalar.activation(K.rms[:, a:b], K.rms[:, a:b], ACT.Exp, scale=-0.5).then_inc(N.rstd, 1)

    if sums == SUMS_FIRST:
        for k in range(KT):
            square(0, k)
        split_hi(K, e, 0, 0)
    rms(0)
    for c, (a, b) in enumerate(PIECES):
        for k in range(KT):
            n = KT * c + k
            if sums == SUMS_FIRST and c + 1 < NPC:
                square(c + 1, k)
            e.wait_ge(N.n32, n + 1)
            nc.scalar.copy(K.nh[:, k, a:b], K.nrm[:, n % 4, :b - a]).then_inc(N.hi, 1)
            if c + 1 < NPC and k == (KT - 1 if sums == SUMS_FIRST else 3):
                rms(c + 1)


def norm_lo(K, e, eng, N, n, done):
    c, k = divmod(n, KT)
    a, b = PIECES[c]
    e.wait_ge(N.hi, n + 1)
    eng.tensor_tensor(K.nl[:, k, a:b], K.nrm[:, n % 4, :b - a], K.nh[:, k, a:b].bitcast(F32),
                      ALU.subtract).then_inc(done, 1)


def norm_dve(K, e, N, gain):
    for c, (a, b) in enumerate(PIECES):
        e.wait_ge(N.rstd, c + 1)
        for k in range(KT):
            n = KT * c + k
            if k % 2:
                wait(e, N.lo_odd, (n - 3) // 2)
            else:
                wait(e, N.lo, n // 2 - 1)
            K.nc.vector.scalar_tensor_tensor(out=K.nrm[:, n % 4, :b - a], in0=K.x[:, k, a:b],
                                             scalar=K.vec[:, gain + k:gain + k + 1],
                                             in1=K.rms[:, a:b], op0=ALU.mult,
                                             op1=ALU.mult).then_inc(N.n32, 1)
            if k % 2:
                norm_lo(K, e, K.nc.vector, N, n - 1, N.lo)


def norm_pool(K, e, N):
    for n in range(1, NPC * KT, 2):
        norm_lo(K, e, K.nc.gpsimd, N, n, N.lo_odd)


def wait_normed(e, N, j, k):
    n = KT * j + k
    e.wait_ge(N.lo_odd if k % 2 else N.lo, n // 2 + 1)


FFN_HEAD = [("up", 0), ("up", 1), ("up", 2), ("up", 3), ("down", 0)]
FFN_BODY = [("up", 4), ("up", 5), ("down", 1), ("up", 6), ("up", 7), ("down", 2)]
FFN_TAIL = [("up", 20), ("up", 21), ("down", 9), ("down", 10)]
FFN_LOOPS = 4
DN = KT * NPC


def ffn_steps(e, run):
    prev = None
    n = 0
    for kind, c in FFN_HEAD:
        run(None, n, kind, c, prev)
        prev = (kind, c)
        n += 1
    with e.Fori(0, FFN_LOOPS) as i:
        prev = ("down", 0)
        for j, (kind, c) in enumerate(FFN_BODY):
            run(i, n + j, kind, c, prev)
            prev = (kind, c)
    n += FFN_LOOPS * len(FFN_BODY)
    prev = ("down", 8)
    for kind, c in FFN_TAIL:
        run(None, n, kind, c, prev)
        prev = (kind, c)
        n += 1


def ffn_step_done(K, e, N, i, step):
    kind, c = step
    if kind == "up":
        e.wait_ge(N.up_mm, at(i, 4 * NPC, NPC * (c + 1)))
    else:
        e.wait_ge(N.down_mm, at(i, 2 * DN, DN * (c + 1)))


def ffn_pe(K, e, N, base):
    def run(i, n, kind, c, before):
        S = at(i, 6, base + n)
        slot = (base + n) % 2
        e.wait_ge(K.w_lo, at(i, 12, 2 * (base + n + 1)))
        if kind == "up":
            whi = K.whi[:, slot].rearrange("p (m k n) -> p m k n", m=2, k=KT)
            wlo = K.wlo[:, slot].rearrange("p (m k n) -> p m k n", m=2, k=KT)
            for j, (a, b) in enumerate(PIECES):
                p = at(i, 4 * NPC, NPC * c + j)
                par = (NPC * c + j) % 2
                for m, done, free in ((0, N.gate_mm, N.silu), (1, N.up_mm, N.h32)):
                    wait(e, free, p - 1)
                    for k in range(KT):
                        if i is None and c == 0 and m == 0:
                            wait_normed(e, N, j, k)
                        mm = three(K, K.ps[:, 2 * m + par, :b - a], whi[:, m, k], wlo[:, m, k],
                                   K.nh[:, k, a:b], K.nl[:, k, a:b], k == 0, k == KT - 1)
                    mm.then_inc(done, 1)
        else:
            whi = K.whi[:, slot].rearrange("p (r n) -> p r n", r=2)
            wlo = K.wlo[:, slot].rearrange("p (r n) -> p r n", r=2)
            e.wait_ge(N.hlo, at(i, 4 * NPC, 2 * NPC * (c + 1)))
            for d in range(KT):
                for j, (a, b) in enumerate(PIECES):
                    o = NPC * d + j
                    q = at(i, 2 * DN, DN * c + o)
                    wait(e, N.x_upd, q - 3)
                    for r in range(2):
                        mm = three(K, K.ps[:, 4 + o % 4, :b - a], whi[:, r, d * P:(d + 1) * P],
                                   wlo[:, r, d * P:(d + 1) * P], K.hh[:, c % 2, r, a:b],
                                   K.hl[:, c % 2, r, a:b], r == 0, r == 1)
                    mm.then_inc(N.down_mm, 1)
    ffn_steps(e, run)


def ffn_act(K, e, N, base, follow=None):
    nc = K.nc

    def hi(i, c, j):
        a, b = PIECES[j]
        p = NPC * c + j
        e.wait_ge(N.h32, at(i, 4 * NPC, p + 1))
        nc.scalar.copy(K.hh[:, (c // 2) % 2, c % 2, a:b], K.h32[:, p % 2, :b - a]).then_inc(N.hhi, 1)

    def run(i, n, kind, c, before):
        if before is None:
            K.before_split_act(e, N)
        else:
            ffn_step_done(K, e, N, i, before)
        if base + n + 1 < NSTEPS:
            split_hi(K, e, at(i, 6, base + n + 1), (base + n + 1) % 2)
        if kind == "up":
            for j, (a, b) in enumerate(PIECES):
                p = at(i, 4 * NPC, NPC * c + j)
                e.wait_ge(N.gate_mm, p + 1)
                wait(e, N.h32, p - 1)
                nc.scalar.activation(K.sg[:, (NPC * c + j) % 2, :b - a],
                                     K.ps[:, (NPC * c + j) % 2, :b - a], ACT.Silu).then_inc(N.silu, 1)
                if j:
                    hi(i, c, j - 1)
            hi(i, c, NPC - 1)
        elif follow and n == FFN_STEPS - 1:
            nc.scalar.preload_act_table_set(LOG_EXP)
            follow_act(K, e, follow, N.x_upd, DN * c)
    ffn_steps(e, run)


def ffn_dve(K, e, N, base):
    nc = K.nc

    def lo(i, c, j):
        a, b = PIECES[j]
        p = NPC * c + j
        e.wait_ge(N.hhi, at(i, 4 * NPC, p + 1))
        nc.vector.tensor_tensor(K.hl[:, (c // 2) % 2, c % 2, a:b], K.h32[:, p % 2, :b - a],
                                K.hh[:, (c // 2) % 2, c % 2, a:b].bitcast(F32),
                                ALU.subtract).then_inc(N.hlo, 1)

    def run(i, n, kind, c, before):
        def split(halves):
            if base + n + 1 < NSTEPS:
                split_lo(K, e, at(i, 6, base + n + 1), (base + n + 1) % 2, halves)

        if kind == "up":
            split((0, 1))
            for j, (a, b) in enumerate(PIECES):
                p = at(i, 4 * NPC, NPC * c + j)
                e.wait_ge(N.silu, p + 1)
                e.wait_ge(N.up_mm, p + 1)
                wait(e, N.hlo, p - 1)
                nc.vector.tensor_tensor(K.h32[:, (NPC * c + j) % 2, :b - a],
                                        K.sg[:, (NPC * c + j) % 2, :b - a],
                                        K.ps[:, 2 + (NPC * c + j) % 2, :b - a],
                                        ALU.mult).then_inc(N.h32, 1)
                if j:
                    lo(i, c, j - 1)
            lo(i, c, NPC - 1)
        else:
            for d in range(KT):
                for j, (a, b) in enumerate(PIECES):
                    o = NPC * d + j
                    q = at(i, 2 * DN, DN * c + o)
                    e.wait_ge(N.down_mm, q + 1)
                    nc.vector.scalar_tensor_tensor(out=K.x[:, d, a:b], in0=K.ps[:, 4 + o % 4, :b - a],
                                                   scalar=0.5, in1=K.x[:, d, a:b], op0=ALU.mult,
                                                   op1=ALU.add).then_inc(N.x_upd, 1)
                if d in (2, 4):
                    split((d // 4,))
    ffn_steps(e, run)


def proj_tiles():
    for t, s in enumerate(IN_PLAN):
        if not isinstance(s, str):
            for m, name in enumerate(s):
                yield t, name, m, IN_START[t] + NPC * m


def proj_pe(K, e, M, t):
    S = BASE_IN + t
    e.wait_ge(K.w_lo, 2 * (S + 1))
    plan = IN_PLAN[t]
    if isinstance(plan, str):
        whi = K.whi[:, S % 2].rearrange("p (k n) -> p k n", k=KT)
        wlo = K.wlo[:, S % 2].rearrange("p (k n) -> p k n", k=KT)
        for j, (a, r) in enumerate(TILES):
            n = IN_START[t] + j
            e.wait_ge(M.proj_read, max(n - 3, 1))
            for k in range(KT):
                mm = three(K, K.ps[:r, n % 4, :256], whi[:, k], wlo[:, k], K.nh[:, k, a:a + r],
                           K.nl[:, k, a:a + r], k == 0, k == KT - 1, token_major=True)
            mm.then_inc(M.proj_mm, 1)
        return
    whi = K.whi[:, S % 2].rearrange("p (m k n) -> p m k n", m=2, k=KT)
    wlo = K.wlo[:, S % 2].rearrange("p (m k n) -> p m k n", m=2, k=KT)
    for m in range(len(plan)):
        for j, (a, b) in enumerate(PIECES):
            n = IN_START[t] + NPC * m + j
            wait(e, M.proj_read, n - 3)
            for k in range(KT):
                if t == 0 and m == 0:
                    wait_normed(e, M.norm, j, k)
                mm = three(K, K.ps[:, n % 4, :b - a], whi[:, m, k], wlo[:, m, k],
                           K.nh[:, k, a:b], K.nl[:, k, a:b], k == 0, k == KT - 1)
            mm.then_inc(M.proj_mm, 1)


def proj_act(K, e, M, t):
    nc = K.nc
    if t == 0:
        K.before_split_proj(e, M)
    else:
        e.wait_ge(M.proj_mm, IN_START[t])
    split_hi(K, e, BASE_IN + t + 1, (BASE_IN + t + 1) % 2)
    plan = IN_PLAN[t]
    if isinstance(plan, str):
        dst = K.fv if plan == "fv" else K.gv
        if plan == "gv":
            e.wait_ge(M.out, 16 * 3)
        for j, (a, r) in enumerate(TILES):
            n = IN_START[t] + j
            e.wait_ge(M.proj_mm, n + 1)
            nc.scalar.copy(dst[:r, j], K.ps[:r, n % 4, :256]).then_inc(M.proj_read, 1)
        return
    for m, name in enumerate(plan):
        for j, (a, b) in enumerate(PIECES):
            n = IN_START[t] + NPC * m + j
            e.wait_ge(M.proj_mm, n + 1)
            src = K.ps[:, n % 4, :b - a]
            if name == "z0" and j == 0:
                e.wait_ge(M.tail, 16)
                e.wait_ge(M.xc, 16)
            if name[0] == "x":
                u = int(name[1:])
                if j == 0:
                    wait(e, M.conv, u - 1)
                    wait(e, M.tail, 2 * (u - 1))
                if j < NPC - 1:
                    nc.scalar.copy(K.raw[:, u % 2, 3 + a:3 + b], src).then_inc(M.proj_read, 1)
                else:
                    nc.scalar.copy(K.raw[:, u % 2, 6 + TP:6 + b], src[:, TP - a:b - a])\
                        .then_inc(M.raw_tail, 1)
                    nc.scalar.copy(K.raw[:, u % 2, 3 + a:3 + TP], src[:, :TP - a]).then_inc(M.proj_read, 1)
                    conv_act(K, e, M, u - 1)
            elif name[0] == "z" or name[:2] == "gg":
                dst = (K.z if name[0] == "z" else K.gg)[:, int(name[-1]), a:b]
                nc.scalar.activation(dst, src, ACT.Silu).then_inc(M.proj_read, 1)
            else:
                if name == "gq" and j == 0:
                    e.wait_ge(M.kout, 16)
                dst = {"fq0": K.fq[:, 0], "fq1": K.fq[:, 1], "fk0": K.fk[:, 0], "fk1": K.fk[:, 1],
                       "small": K.small, "gk": K.gk, "gq": K.gq}[name]
                nc.scalar.copy(dst[:, a:b], src).then_inc(M.proj_read, 1)
    if plan[-1] == "x7":
        conv_act(K, e, M, 7)


def conv_act(K, e, M, u):
    if u < 0:
        return
    e.wait_ge(M.conv, u + 1)
    b = K.vec[:, V_CB + u:V_CB + u + 1]
    K.nc.scalar.activation(K.xc[:, u, :TP], K.acc[:, u % 2, :TP], ACT.Silu, bias=b).then_inc(M.xc, 1)
    K.nc.scalar.activation(K.xc[:, u, TP:], K.acc[:, u % 2, TP + 3:TP + 3 + TS], ACT.Silu,
                           bias=b).then_inc(M.xc, 1)


def conv_dve(K, e, M, t):
    nc = K.nc
    L = T + 3
    for name in IN_PLAN[t]:
        u = int(name[1:])
        e.wait_ge(M.proj_read, IN_START[t] + NPC * (u % 2) + NPC)
        e.wait_ge(M.raw_tail, u + 1)
        e.wait_ge(M.prev, u + 1)
        wait(e, M.xc, 2 * (u - 1))
        acc = K.acc[:, u % 2]
        w = [K.vec[:, V_CW + 4 * u + q:V_CW + 4 * u + q + 1] for q in range(4)]
        M.dve(nc.vector.tensor_scalar(acc, K.raw[:, u % 2, 0:L], w[0], None, ALU.mult))
        for q in (1, 2):
            M.dve(nc.vector.scalar_tensor_tensor(out=acc, in0=K.raw[:, u % 2, q:q + L], scalar=w[q],
                                                 in1=acc, op0=ALU.mult, op1=ALU.add))
        nc.vector.scalar_tensor_tensor(out=acc, in0=K.raw[:, u % 2, 3:3 + L], scalar=w[3], in1=acc,
                                       op0=ALU.mult, op1=ALU.add).then_inc(M.conv, 1)


def conv_pool(K, e, M, out_tail):
    nc = K.nc
    for s in range(2):
        nc.gpsimd.memset(K.raw[:, s, 0:3], 0.0).then_inc(M.pad, 1)
    e.wait_ge(M.pad, 2)
    for u in range(8):
        wait(e, M.conv, u - 1)
        nc.gpsimd.tensor_copy(K.raw[:, u % 2, 3 + TP:6 + TP], K.cprev[:, u]).then_inc(M.prev, 1)
        e.wait_ge(M.raw_tail, u + 1)
        e.wait_ge(M.proj_read, IN_START[CONV_AT] + NPC * (u + 1))
        nc.gpsimd.tensor_copy(K.ctail[:, u, 0], K.raw[:, u % 2, TP:TP + 3]).then_inc(M.tail, 1)
        nc.gpsimd.tensor_copy(K.ctail[:, u, 1], K.raw[:, u % 2, 3 + T:6 + T]).then_inc(M.tail, 1)
    e.wait_ge(M.tail, 16)
    e.dma_start(out_tail, K.ctail[:]).then_inc(M.out, 16)


def softplus_act(K, e, s, a, b):
    e.wait_ge(s.absv, 1)
    K.nc.scalar.activation(a, a, ACT.Exp, scale=-1.0).then_inc(s.e, 1)
    e.wait_ge(s.u, 1)
    K.nc.scalar.activation(b, b, ACT.Ln).then_inc(s.ln, 1)


def softplus_dve(K, e, M, s, v, a, b):
    V = K.nc.vector
    V.scalar_tensor_tensor(out=a, in0=v, scalar=-1.0, in1=v, op0=ALU.mult, op1=ALU.max).then_inc(s.absv, 1)
    e.wait_ge(s.e, 1)
    M.dve(V.tensor_scalar(b, a, 1.0, None, ALU.add))
    V.scalar_tensor_tensor(out=a, in0=b, scalar=-1.0, in1=a, op0=ALU.add, op1=ALU.subtract).then_inc(s.u, 1)
    e.wait_ge(s.ln, 1)
    M.dve(V.tensor_tensor(a, b, a, ALU.subtract))


FOX_UNITS = [(h, j) for h in range(FOX_H) for j in range(NTT)]
NU = len(FOX_UNITS)
BIAS_AT = 4


def bias_bank(it, q):
    return 2 * ((it + 1) % 2) + q % 2




def fox_keys(j):
    return PAST + TS if j == NTT - 1 else P * (j + 1)


def fox_groups(j):
    n = fox_keys(j)
    tiles = [(k, min(P, n - k)) for k in range(0, n, P)]
    return [tiles[g:g + 4] for g in range(0, len(tiles), 4)]


FOX_G = [0]
for _h, _j in FOX_UNITS:
    FOX_G.append(FOX_G[-1] + len(fox_groups(_j)))
FOX_QK = [(n // NPC, PIECES[n % NPC]) for n in range(4 * NPC)]


def fox_tile(K, m):
    return K.fq[:, m] if m < 2 else K.fk[:, m - 2]


def fox_pe(K, e, M):
    nc = K.nc
    for n, (m, (a, b)) in enumerate(FOX_QK):
        e.wait_ge(M.fsq, n + 1)
        wait(e, M.fln, n - 1)
        nc.tensor.matmul(K.ps[:, 4 + n % 2, :b - a], K.b64, K.sq[:, n % 2, :b - a],
                         start=True, stop=True).then_inc(M.fss, 1)

    def bias(h, it):
        wait(e, M.smin, it)
        for q in range(4):
            n = 4 * h + q
            if n == 0:
                e.wait_ge(M.cum, 1)
            wait(e, M.cb, n - 1)
            nc.tensor.matmul(K.ps[:, bias_bank(it, q), :400], K.const[SMALL_FF:SMALL_FF + FOX_H, C_SEL + h * P:C_SEL + (h + 1) * P],
                             K.cum[SMALL_FF:SMALL_FF + FOX_H, 400 * q:400 * q + 400],
                             start=True, stop=True).then_inc(M.cb_mm, 1)

    def scores(u):
        h, j = FOX_UNITS[u]
        a, r = TILES[j]
        o = 64 * (h % 2)
        q = K.fq[o:o + 64, h // 2, a:a + r]
        wait(e, M.smin, u - 1)
        if u == 0 or FOX_UNITS[u - 1][1] == BIAS_AT and h < FOX_H - 1:
            e.wait_ge(M.cb, 4 * (h + 1 + (u > 0)))
        if j < NTT - 1:
            n = fox_keys(j)
            parts = [(k, min(512, n - k), K.fk[o:o + 64, h // 2, k:min(k + 512, n)]) for k in range(0, n, 512)]
        else:
            parts = [(0, PAST, K.kc[o:o + 64, h // 2, :]), (PAST, TS, K.fk[o:o + 64, h // 2, TP:T])]
        for k, n, rhs in parts:
            mm = nc.tensor.matmul(K.psf[:r, 1024 * (u % 2) + k:1024 * (u % 2) + k + n], q, rhs,
                                  start=True, stop=True)
        mm.then_inc(M.s_mm, 1)

    def turn(u):
        h, j = FOX_UNITS[u]
        r = TILES[j][1]
        e.wait_ge(M.p_scaled, u + 1)
        for g, tiles in enumerate(fox_groups(j)):
            n = FOX_G[u] + g
            wait_pt(n - 2)
            for i, (k, w) in enumerate(tiles):
                mm = nc.tensor.transpose(K.ps[:w, 4 + n % 2, i * P:i * P + r], K.pr[:r, u % 3, k:k + w],
                                         K.ident[:r, :r])
            mm.then_inc(M.pt_mm, 1)

    def wait_pt(n):
        if n < 0:
            return
        u = max(v for v in range(NU) if FOX_G[v] <= n)
        if n == FOX_G[u]:
            e.wait_ge(M.pt_a, u + 1)
        else:
            e.wait_ge(M.pt_v, K.second(u) + 1)

    def values(u):
        h, j = FOX_UNITS[u]
        r = TILES[j][1]
        o = 64 * (h % 2)
        e.wait_ge(M.pt_a, u + 1)
        wait(e, M.pt_v, K.second(u + 1))
        wait(e, M.fo, u - 1)
        tiles = [x for g in fox_groups(j) for x in g]
        for i, (k, w) in enumerate(tiles):
            if j == NTT - 1:
                v = K.vc[:, i, 64 * h:64 * h + 64] if i < PAST // P else K.fv[:TS, j, 64 * h:64 * h + 64]
            else:
                v = K.fv[:, i, 64 * h:64 * h + 64]
            mm = nc.tensor.matmul(K.ps[o:o + 64, 6 + u % 2, :r], v, K.pt[:w, u % 2, i, :r],
                                  start=i == 0, stop=i == len(tiles) - 1)
        mm.then_inc(M.o_mm, 1)

    bias(0, -1)
    e.wait_ge(M.fqk, len(FOX_QK))
    e.wait_ge(M.cache, 16 * 3)
    for it in range(NU + 3):
        if it < NU:
            scores(it)
            h, j = FOX_UNITS[it]
            if j == BIAS_AT and h + 1 < FOX_H:
                bias(h + 1, it)
        if 0 <= it - 2 < NU:
            turn(it - 2)
        if 0 <= it - 3 < NU:
            values(it - 3)


def fox_act(K, e, M):
    nc = K.nc
    nc.scalar.preload_act_table_set(LOG_EXP)
    e.wait_ge(M.proj_read, IN_START[FOX_AT])
    softplus_act(K, e, M.sp, K.t1, K.t2)
    for n, (m, (a, b)) in enumerate(FOX_QK):
        wait(e, M.fss, n - 1)
        nc.scalar.activation(K.sq[:, n % 2, :b - a], fox_tile(K, m)[:, a:b], ACT.Square).then_inc(M.fsq, 1)
        if n:
            rstd(K, e, M, n - 1)
    rstd(K, e, M, len(FOX_QK) - 1)

    def bias(h, it):
        for q in range(4):
            n = 4 * h + q
            e.wait_ge(M.cb_mm, n + 1)
            nc.scalar.copy(K.cb[:, h % 2, 400 * q:400 * q + 400], K.ps[:, bias_bank(it, q), :400]).then_inc(M.cb, 1)

    def turned(u):
        h, j = FOX_UNITS[u]
        r = TILES[j][1]
        e.wait_ge(M.pt_mm, FOX_G[u] + 1)
        wait(e, M.o_mm, u - 1)
        n = len(fox_groups(j)[0])
        nc.scalar.copy(K.pt[:, u % 2, :n, :r],
                       K.ps[:, 4 + FOX_G[u] % 2].rearrange("p (n q) -> p n q", q=P)[:, :n, :r])\
            .then_inc(M.pt_a, 1)

    bias(0, -1)
    for it in range(NU + 2):
        if it < NU:
            h, j = FOX_UNITS[it]
            r = TILES[j][1]
            n = fox_keys(j)
            e.wait_ge(M.smin, it + 1)
            nc.scalar.activation(K.pr[:r, it % 3, :n], K.pr[:r, it % 3, :n], ACT.Exp, bias=K.mn[:r, it % 3:it % 3 + 1],
                                 scale=-1.0, accum_out=K.rs[:r, it % 3:it % 3 + 1]).then_inc(M.p_exp, 1)
            if j == BIAS_AT and h + 1 < FOX_H:
                bias(h + 1, it)
        if it >= 2:
            turned(it - 2)


def rstd(K, e, M, n):
    a, b = FOX_QK[n][1]
    e.wait_ge(M.fss, n + 1)
    wait(e, M.frs, n)
    K.nc.scalar.activation(K.lnv[:, :b - a], K.ps[:, 4 + n % 2, :b - a], ACT.Ln, bias=K.eps[:, 0:1],
                           scale=1.0 / FOX_D).then_inc(M.fln, 1)
    e.wait_ge(M.fln, n + 1)
    wait(e, M.fqk, n - 1)
    K.nc.scalar.activation(K.n32[:, n % 2, :b - a], K.lnv[:, :b - a], ACT.Exp, scale=-0.5).then_inc(M.frs, 1)


def fox_dve(K, e, M):
    nc = K.nc
    V = nc.vector
    e.wait_ge(M.proj_read, IN_START[3])
    e.wait_ge(M.x_out, 16)
    M.dve(V.tensor_scalar(K.small[:], K.small[:], K.vec[:, V_SB:V_SB + 1], None, ALU.add))
    softplus_dve(K, e, M, M.sp, K.small[:], K.t1, K.t2)
    f = slice(SMALL_FF, SMALL_FF + FOX_H)
    g = slice(SMALL_DT, SMALL_DT + SSD_H)
    V.scalar_tensor_tensor(out=K.small[f, :], in0=K.small[f, :], scalar=0.0, in1=K.t1[f, :],
                           op0=ALU.min, op1=ALU.subtract).then_inc(M.logf, 1)
    M.dve(V.scalar_tensor_tensor(out=K.small[g, :], in0=K.small[g, :], scalar=0.0, in1=K.t1[g, :],
                                 op0=ALU.max, op1=ALU.add))
    e.wait_ge(M.logf, 1)
    e.wait_ge(M.cache, 16 * 3)
    ones = K.t2[f, :TP]
    M.dve(V.memset(ones, 1.0))
    M.dve(V.tensor_tensor_scan(K.cum[f, 0:TP], ones, K.small[f, 0:TP], 0.0, ALU.mult, ALU.add))
    M.dve(V.tensor_tensor_scan(K.cum[f, TP:TP + PAST], ones[:, :PAST], K.lfc[f, :], 0.0, ALU.mult, ALU.add))
    V.tensor_tensor_scan(K.cum[f, TP + PAST:], ones[:, :TS], K.small[f, TP:T],
                         K.cum[f, TP + PAST - 1:TP + PAST], ALU.mult, ALU.add).then_inc(M.cum, 1)
    for n, (m, (a, b)) in enumerate(FOX_QK):
        gain = V_QN if m < 2 else V_KN
        e.wait_ge(M.frs, n + 1)
        V.scalar_tensor_tensor(out=fox_tile(K, m)[:, a:b], in0=fox_tile(K, m)[:, a:b],
                               scalar=K.vec[:, gain:gain + 1], in1=K.n32[:, n % 2, :b - a],
                               op0=ALU.mult, op1=ALU.mult).then_inc(M.fqk, 1)
    for it in range(NU + 3):
        if it < NU:
            h, j = FOX_UNITS[it]
            r = TILES[j][1]
            n = fox_keys(j)
            e.wait_ge(M.s_mm, it + 1)
            e.wait_ge(M.cb, 4 * (h + 1))
            if it >= 3:
                e.wait_ge(M.pt_mm, FOX_G[it - 2])
            s = K.psf[:r, 1024 * (it % 2):1024 * (it % 2) + n]
            M.dve(V.tensor_tensor(s[:, n - r:n], s[:, n - r:n], K.mqk[:r, :r], ALU.add))
            c0 = 0 if j < NTT - 1 else TP
            V.tensor_tensor_reduce(out=K.pr[:r, it % 3, :n], in0=s, in1=K.cb[:r, h % 2, c0:c0 + n],
                                   scale=-0.125, scalar=3e38, op0=ALU.add, op1=ALU.min,
                                   accum_out=K.mn[:r, it % 3:it % 3 + 1]).then_inc(M.smin, 1)
        if 1 <= it <= NU:
            u = it - 1
            r = TILES[FOX_UNITS[u][1]][1]
            e.wait_ge(M.p_exp, u + 1)
            wait(e, M.p_scaled, u - 2)
            V.reciprocal(K.ri[:r, u % 3:u % 3 + 1], K.rs[:r, u % 3:u % 3 + 1]).then_inc(M.rinv, 1)
        if 0 <= it - 2 < NU:
            u = it - 2
            h, j = FOX_UNITS[u]
            r = TILES[j][1]
            gs = fox_groups(j)
            if len(gs) > 1:
                n = FOX_G[u] + 1
                e.wait_ge(M.pt_mm, n + 1)
                wait(e, M.o_mm, u - 1)
                m, w = len(gs[1]), gs[1][0][1]
                V.tensor_copy(K.pt[:w, u % 2, 4:4 + m, :r],
                              K.ps[:w, 4 + n % 2].rearrange("p (n q) -> p n q", q=P)[:, :m, :r])\
                    .then_inc(M.pt_v, 1)
        if 0 <= it - 3 < NU:
            u = it - 3
            h, j = FOX_UNITS[u]
            a, r = TILES[j]
            o = 64 * (h % 2)
            e.wait_ge(M.o_mm, u + 1)
            if u == 0:
                e.wait_ge(M.kout, 16)
            V.tensor_copy(K.fq[o:o + 64, h // 2, a:a + r], K.ps[o:o + 64, 6 + u % 2, :r])\
                .then_inc(M.fo, 1)


def fox_pool(K, e, M, outs):
    nc = K.nc
    e.wait_ge(M.proj_read, IN_START[FOX_AT])
    for j in range(2):
        src = K.fv[:, :TP // P] if j == 0 else K.fv[:TS, TP // P:TP // P + 1]
        e.dma_start(outs["v"][j], src).then_inc(M.out, 16)
    e.wait_ge(M.logf, 1)
    e.dma_start(outs["logf"], K.small[SMALL_FF:SMALL_FF + FOX_H, :]).then_inc(M.out, 16)
    e.wait_ge(M.fqk, len(FOX_QK))
    e.dma_start(outs["k"], K.fk[:]).then_inc(M.kout, 16)
    for u, (h, j) in enumerate(FOX_UNITS):
        r = TILES[j][1]
        n = fox_keys(j)
        e.wait_ge(M.rinv, u + 1)
        nc.gpsimd.tensor_scalar(K.pr[:r, u % 3, :n], K.pr[:r, u % 3, :n], K.ri[:r, u % 3:u % 3 + 1], 1.0,
                                ALU.mult, ALU.mult).then_inc(M.p_scaled, 1)


GLA_L = 64
GCH = T // GLA_L


def gla_pe(K, e, M):
    nc = K.nc
    e.wait_ge(M.proj_read, IN_START[GLA_AT])
    e.wait_ge(M.fo, NU)
    for j, (a, b) in enumerate(PIECES):
        nc.tensor.matmul(K.ps[:, 4 + j, :b - a], K.const[:GLA_R, C_SEL:C_SEL + P], K.small[:GLA_R, a:b],
                         start=True, stop=True).then_inc(M.g_mm, 1)
    for j, (a, r) in enumerate(TILES):
        if j == 0:
            e.wait_ge(M.kend, 1)
        wait(e, M.kt_read, j - 1)
        nc.tensor.transpose(K.ps[:r, 4 + j % 2, :P], K.ge[:, a:a + r], K.ident).then_inc(M.kt_mm, 1)
    e.wait_ge(M.kt_read, NTT)
    e.wait_ge(M.gqk, 1)
    for j, (a, r) in enumerate(TILES):
        wait(e, M.att, j)
        for h in range(GLA_H):
            o = GLA_K * h
            mm = nc.tensor.matmul(K.ps[:r, h, :r], K.gk[o:o + GLA_K, a:a + r], K.gq[o:o + GLA_K, a:a + r],
                                  start=True, stop=True)
        mm.then_inc(M.att_mm, 1)
        for s in range(r // GLA_L):
            c = 2 * j + s
            o = GLA_L * s
            wait(e, M.st_read, c - 1)
            nc.tensor.matmul(K.ps[:, 6 + s, :256], K.kt[o:o + GLA_L, j], K.gv[o:o + GLA_L, j],
                             start=True, stop=True).then_inc(M.st_mm, 1)
        wait(e, M.go_read, j - 1)
        out = K.ps[:, 4 + j % 2, :256].rearrange("p (t q) -> p t q", t=2)
        first = True
        for s in range(r // GLA_L):
            c = 2 * j + s
            e.wait_ge(M.S, c + 1)
            for t in range(2):
                nc.tensor.matmul(out[:, t, GLA_L * s:GLA_L * s + GLA_L], K.S[:, c % 4, P * t:P * t + P],
                                 K.gq[:, a + GLA_L * s:a + GLA_L * s + GLA_L], start=first, stop=False,
                                 skip_group_check=True)
                first = False
        e.wait_ge(M.att, j + 1)
        for h in range(GLA_H):
            o = 64 * (h % 2)
            mm = nc.tensor.matmul(out[o:o + 64, h // 2, :r], K.gv[:r, j, 64 * h:64 * h + 64], K.attn[:r, j % 2, h, :r],
                                  start=False, stop=h == GLA_H - 1, skip_group_check=True)
        mm.then_inc(M.go_mm, 1)
    e.wait_ge(M.go_read, NTT)
    for n in range(2 * NPC):
        a, b = PIECES[n % NPC]
        e.wait_ge(M.gsq, n + 1)
        wait(e, M.gln, n - 1)
        nc.tensor.matmul(K.ps[:, 4 + n % 2, :b - a], K.b64, K.sq[:, n % 2, :b - a],
                         start=True, stop=True).then_inc(M.gss, 1)


def gla_act(K, e, M):
    nc = K.nc
    nc.scalar.preload_act_table_set(LOG_EXP)
    softplus_act(K, e, M.gsp, K.ga[:], K.gb[:])
    e.wait_ge(M.bcum, 1)
    nc.scalar.activation(K.ga[:], K.ge[:], ACT.Exp).then_inc(M.eb, 1)
    nc.scalar.activation(K.gb[:], K.ge[:], ACT.Exp, scale=-1.0).then_inc(M.enb, 1)
    e.wait_ge(M.bdiff, 1)
    nc.scalar.activation(K.gd[:], K.gd[:], ACT.Exp).then_inc(M.ebd, 1)
    for j, (a, r) in enumerate(TILES):
        e.wait_ge(M.kt_mm, j + 1)
        nc.scalar.copy(K.kt[:r, j], K.ps[:r, 4 + j % 2, :P]).then_inc(M.kt_read, 1)
    for j, (a, r) in enumerate(TILES):
        e.wait_ge(M.go_mm, j + 1)
        nc.scalar.copy(K.go[:, :, a:a + r], K.ps[:, 4 + j % 2, :256].rearrange("p (t q) -> p t q", t=2)[:, :, :r])\
            .then_inc(M.go_read, 1)
    e.wait_ge(M.go_read, NTT)
    for n in range(2 * NPC + 1):
        if n < 2 * NPC:
            a, b = PIECES[n % NPC]
            wait(e, M.gss, n - 1)
            nc.scalar.activation(K.sq[:, n % 2, :b - a], K.go[:, n // NPC, a:b], ACT.Square).then_inc(M.gsq, 1)
        if n:
            m = n - 1
            a, b = PIECES[m % NPC]
            e.wait_ge(M.gss, m + 1)
            wait(e, M.grs, m)
            nc.scalar.activation(K.lnv[:, :b - a], K.ps[:, 4 + m % 2, :b - a], ACT.Ln, bias=K.eps[:, 0:1],
                                 scale=1.0 / GLA_V).then_inc(M.gln, 1)
            e.wait_ge(M.gln, m + 1)
            wait(e, M.gnorm, m - 1)
            nc.scalar.activation(K.n32[:, m % 2, :b - a], K.lnv[:, :b - a], ACT.Exp, scale=-0.5).then_inc(M.grs, 1)


def gla_dve(K, e, M):
    nc = K.nc
    V = nc.vector
    ch = lambda t: t[:].rearrange("p (c l) -> p c l", l=GLA_L)
    e.wait_ge(M.g_mm, NPC)
    for j, (a, b) in enumerate(PIECES):
        M.dve(V.tensor_scalar(K.gd[:, a:b], K.ps[:, 4 + j, :b - a], K.vec[:, V_GB:V_GB + 1], None, ALU.add))
    softplus_dve(K, e, M, M.gsp, K.gd[:], K.ga[:], K.gb[:])
    M.dve(V.scalar_tensor_tensor(out=K.gd[:], in0=K.gd[:], scalar=0.0, in1=K.ga[:], op0=ALU.min, op1=ALU.subtract))
    M.dve(V.tensor_scalar(K.gd[:], K.gd[:], 1.0 / GLA_TAU, None, ALU.mult))
    M.dve(V.memset(K.ga[:], 1.0))
    M.dve(V.memset(ch(K.ga)[:, :, 0:1], 0.0))
    V.tensor_tensor_scan(K.ge[:], K.ga[:], K.gd[:], 0.0, ALU.mult, ALU.add).then_inc(M.bcum, 1)
    e.wait_ge(M.bcum, 1)
    V.tensor_tensor(ch(K.gd), ch(K.ge)[:, :, GLA_L - 1:GLA_L].to_broadcast([P, GCH, GLA_L]), ch(K.ge),
                    ALU.subtract).then_inc(M.bdiff, 1)
    e.wait_ge(M.eb, 1)
    M.dve(V.tensor_copy(K.glast[:], ch(K.ga)[:, :, GLA_L - 1]))
    M.dve(V.scalar_tensor_tensor(out=K.gq[:], in0=K.gq[:], scalar=float(GLA_K) ** -0.5, in1=K.ga[:],
                                 op0=ALU.mult, op1=ALU.mult))
    e.wait_ge(M.ebd, 1)
    e.wait_ge(M.enb, 1)
    V.tensor_tensor(K.ge[:], K.gk[:], K.gd[:], ALU.mult).then_inc(M.kend, 1)
    e.wait_ge(M.kend, 1)
    V.tensor_tensor(K.gk[:], K.gk[:], K.gb[:], ALU.mult).then_inc(M.gqk, 1)
    M.dve(V.memset(K.attn[:], 0.0))
    V.memset(K.S[:, 0], 0.0).then_inc(M.S, 1)
    e.wait_ge(M.S, 1)
    for j, (a, r) in enumerate(TILES):
        e.wait_ge(M.att_mm, j + 1)
        wait(e, M.go_mm, j - 1)
        V.copy_predicated(K.attn[:r, j % 2, :, :r], K.gmask[:r, :r].rearrange("p (o q) -> p o q", o=1)
                          .to_broadcast([r, GLA_H, r]), K.ps[:r, 0:GLA_H, :r]).then_inc(M.att, 1)
        for s in range(r // GLA_L):
            c = 2 * j + s
            e.wait_ge(M.st_mm, c + 1)
            V.tensor_tensor(K.gst[:], K.ps[:, 6 + s, :256], K.bmask, ALU.mult).then_inc(M.st_read, 1)
            e.wait_ge(M.st_read, c + 1)
            if c == TP // GLA_L - 1:
                M.dve(V.scalar_tensor_tensor(out=K.Sp[:], in0=K.S[:, c % 4], scalar=K.glast[:, c:c + 1],
                                             in1=K.gst[:], op0=ALU.mult, op1=ALU.add))
                e.wait_ge(M.go_mm, (c - 3) // 2 + 1)
                e.wait_ge(M.Sin, 16 * GLA_H)
                V.tensor_copy(K.S[:, (c + 1) % 4], K.Sin[:]).then_inc(M.S, 1)
                e.wait_ge(M.S, c + 2)
            elif c == GCH - 1:
                V.scalar_tensor_tensor(out=K.Ss[:], in0=K.S[:, c % 4], scalar=K.glast[:, c:c + 1],
                                       in1=K.gst[:], op0=ALU.mult, op1=ALU.add).then_inc(M.S_end, 1)
            else:
                if c >= 3:
                    e.wait_ge(M.go_mm, (c - 3) // 2 + 1)
                V.scalar_tensor_tensor(out=K.S[:, (c + 1) % 4], in0=K.S[:, c % 4], scalar=K.glast[:, c:c + 1],
                                       in1=K.gst[:], op0=ALU.mult, op1=ALU.add).then_inc(M.S, 1)
                e.wait_ge(M.S, c + 2)
    for n in range(2 * NPC):
        a, b = PIECES[n % NPC]
        e.wait_ge(M.grs, n + 1)
        o = K.go[:, n // NPC, a:b]
        V.scalar_tensor_tensor(out=o, in0=o, scalar=K.vec[:, V_GN:V_GN + 1], in1=K.n32[:, n % 2, :b - a],
                               op0=ALU.mult, op1=ALU.mult).then_inc(M.gnorm, 1)
        e.wait_ge(M.gnorm, n + 1)
        V.tensor_tensor(K.gg[:, n // NPC, a:b], o, K.gg[:, n // NPC, a:b], ALU.mult).then_inc(M.gout, 1)


def gla_pool(K, e, M, outs):
    e.wait_ge(M.S_end, 1)
    for j, src in enumerate((K.Sp, K.Ss)):
        for h in range(GLA_H):
            o = GLA_K * h
            e.dma_start(outs["gla"][j, o:o + GLA_K], src[o:o + GLA_K, 64 * h:64 * h + 64]).then_inc(M.out, 16)


CB_BANKS = (4, 7)


def ssd_pe(K, e, M):
    nc = K.nc
    g = slice(SMALL_DT, SMALL_DT + SSD_H)
    e.wait_ge(M.proj_read, IN_START[IN_STEPS])
    e.wait_ge(M.acum, 1)
    e.wait_ge(M.xc, 16)
    e.wait_ge(M.H, 1)

    def front(j):
        a, r = TILES[j]
        wait(e, M.seg, j)
        wait(e, M.ea, j)
        wait(e, M.de0, j)
        for h in range(SSD_H):
            mm = nc.tensor.matmul(K.psf[:, P * h:P * h + r], K.const[g, C_SEL + P * h:C_SEL + P * h + P],
                                  K.adt[g, a:a + r], start=True, stop=True)
        mm.then_inc(M.a_mm, 1)
        wait(e, M.b_read, j)
        wait(e, M.sm_read, j)
        for u in range(2):
            nc.tensor.transpose(K.ps[:r, 3, P * u:P * u + P], K.xc[:, 4 + u, a:a + r], K.ident)
        nc.tensor.transpose(K.ps[:r, 3, 256:264], K.adt[g, a:a + r], K.ident[g, g])
        nc.tensor.transpose(K.ps[:r, 3, 264:272], K.small[g, a:a + r], K.ident[g, g]).then_inc(M.b_mm, 1)
        wait(e, M.m, j - 1)
        for u in range(2):
            mm = nc.tensor.matmul(K.ps[:r, CB_BANKS[j % 2], P * u:P * u + r], K.xc[:, 4 + u, a:a + r],
                                  K.xc[:, 6 + u, a:a + r], start=True, stop=True)
        mm.then_inc(M.cb2_mm, 1)
        wait(e, M.x_read, j)
        for u in range(4):
            mm = nc.tensor.transpose(K.ps[:r, 2, P * u:P * u + P], K.xc[:, u, a:a + r], K.ident)
        mm.then_inc(M.x_mm, 1)

    def back(j):
        a, r = TILES[j]
        wait(e, M.y1, j)
        e.wait_ge(M.cea, j + 1)
        wait(e, M.hst_read, j)
        if j == NTT - 1:
            e.wait_ge(M.H, 2)
        y = K.ps[:, 5].rearrange("p (t q) -> p t q", t=4)
        for h in range(SSD_H):
            o = 64 * (h % 2)
            mm = nc.tensor.matmul(y[o:o + 64, h // 2, :r], K.H[:, 64 * h:64 * h + 64], K.cea[:, j % 2, h, :r],
                             start=h < 2, stop=False, skip_group_check=True)
        mm.then_inc(M.h_read, 1)
        e.wait_ge(M.b_read, j + 1)
        e.wait_ge(M.x_read, j + 1)
        for u in range(2):
            mm = nc.tensor.matmul(K.ps[:, 6, 256 * u:256 * u + 256], K.btok[:r, P * u:P * u + P],
                                  K.xde[:r, 256 * u:256 * u + 256], start=True, stop=True)
        mm.then_inc(M.hst_mm, 1)
        e.wait_ge(M.m, j + 1)
        e.wait_ge(M.xdt, j + 1)
        for h in range(SSD_H):
            o = 64 * (h % 2)
            mm = nc.tensor.matmul(y[o:o + 64, h // 2, :r], K.xdt[:r, 64 * h:64 * h + 64], K.seg[:r, j % 2, h, :r],
                                  start=False, stop=h >= 6, skip_group_check=True)
        mm.then_inc(M.y_mm, 1)

    front(0)
    for j in range(NTT):
        if j + 1 < NTT:
            front(j + 1)
        back(j)
    for n in range(2 * NPC):
        a, b = PIECES[n % NPC]
        for u in range(2):
            m = 2 * n + u
            e.wait_ge(M.ysq, m + 1)
            if u == 0:
                wait(e, M.yln, n - 1)
            nc.tensor.matmul(K.ps[:, n % 2, :b - a], K.ones, K.sq[:, m % 2, :b - a],
                             start=u == 0, stop=u == 1).then_inc(M.yss, 1)


def ssd_act(K, e, M):
    nc = K.nc
    nc.scalar.preload_act_table_set(LOG_EXP)
    nc.scalar.activation(K.eal[SMALL_DT:SMALL_DT + SSD_H, 0:1], K.vec[SMALL_DT:SMALL_DT + SSD_H, V_AL:V_AL + 1],
                         ACT.Exp).then_inc(M.ealog, 1)
    for j, (a, r) in enumerate(TILES):
        e.wait_ge(M.de0, j + 1)
        nc.scalar.activation(K.de[:r, 0:8], K.de[:r, 0:8], ACT.Exp).then_inc(M.de1, 1)
        e.wait_ge(M.seg, j + 1)
        wait(e, M.cea, j - 1)
        wait(e, M.hupd, j - 1)
        nc.scalar.activation(K.ea[:, j % 2, :, :r],
                             K.psf[:, :1024].rearrange("p (h q) -> p h q", h=SSD_H)[:, :, :r],
                             ACT.Exp).then_inc(M.ea, 1)
        nc.scalar.activation(K.seg[:r, j % 2, :, :r], K.seg[:r, j % 2, :, :r], ACT.Exp).then_inc(M.eseg, 1)
        wait(e, M.hst_mm, j)
        nc.scalar.copy(K.btok[:r, :], K.ps[:r, 3, 0:256]).then_inc(M.b_read, 1)
    for n in range(2 * NPC + 1):
        if n < 2 * NPC:
            a, b = PIECES[n % NPC]
            for u in range(2):
                m = 2 * n + u
                e.wait_ge(M.y2, NTT)
                wait(e, M.yss, m - 1)
                nc.scalar.activation(K.sq[:, m % 2, :b - a], K.z[:, 2 * (n // NPC) + u, a:b], ACT.Square)\
                    .then_inc(M.ysq, 1)
        if n:
            m = n - 1
            a, b = PIECES[m % NPC]
            e.wait_ge(M.yss, 2 * (m + 1))
            wait(e, M.yrs, m)
            nc.scalar.activation(K.lnv[:, :b - a], K.ps[:, m % 2, :b - a], ACT.Ln, bias=K.eps[:, 0:1],
                                 scale=1.0 / 256).then_inc(M.yln, 1)
            e.wait_ge(M.yln, m + 1)
            wait(e, M.ynorm, 2 * (m - 1))
            nc.scalar.activation(K.n32[:, m % 2, :b - a], K.lnv[:, :b - a], ACT.Exp, scale=-0.5).then_inc(M.yrs, 1)


def ssd_prep_dve(K, e, M):
    V = K.nc.vector
    g = slice(SMALL_DT, SMALL_DT + SSD_H)
    e.wait_ge(M.ealog, 1)
    M.dve(V.tensor_scalar(K.pre[g, 0], K.small[g, :], K.eal[g, 0:1], -1.0, ALU.mult, ALU.mult))
    M.dve(V.memset(K.pre[g, 1], 1.0))
    M.dve(V.memset(K.pre[g, 1, 0:T:P], 0.0))
    V.tensor_tensor_scan(K.adt[g, :], K.pre[g, 1], K.pre[g, 0], 0.0, ALU.mult, ALU.add).then_inc(M.acum, 1)


def ssd_dve(K, e, M):
    nc = K.nc
    V = nc.vector
    e.wait_ge(M.xc, 16)
    e.wait_ge(M.proj_mm, IN_START[IN_STEPS])
    ssd_prep_dve(K, e, M)
    V.memset(K.H[:], 0.0).then_inc(M.H, 1)
    pa = K.psf[:, :1024].rearrange("p (h q) -> p h q", h=SSD_H)
    heads = lambda t, r: t[:r].rearrange("p (h q) -> p h q", h=SSD_H)
    hv = K.H[:].rearrange("p (h q) -> p h q", h=SSD_H)

    def decays(j):
        a, r = TILES[j]
        e.wait_ge(M.a_mm, j + 1)
        e.wait_ge(M.b_mm, j + 1)
        V.tensor_copy(K.tk[:r, :], K.ps[:r, 3, 256:272]).then_inc(M.sm_read, 1)
        e.wait_ge(M.sm_read, j + 1)
        V.tensor_tensor(K.de[:r, 0:8], pa[:r, :, r - 1], K.tk[:r, 0:8], ALU.subtract).then_inc(M.de0, 1)
        for h in range(SSD_H):
            ins = V.scalar_tensor_tensor(out=K.seg[:r, j % 2, h, :r], in0=pa[:r, h, :r], scalar=K.tk[:r, h:h + 1],
                                         in1=K.msl[:r, :r], op0=ALU.subtract, op1=ALU.add)
        ins.then_inc(M.seg, 1)

    def state(j):
        a, r = TILES[j]
        e.wait_ge(M.h_read, j + 1)
        dst = K.Hp if j == TP // P - 1 else K.Hs if j == NTT - 1 else K.H
        V.tensor_tensor(K.ht[:].rearrange("p (h q) -> p h q", h=SSD_H), hv,
                        K.ea[:, j % 2, :, r - 1:r].to_broadcast([P, SSD_H, SSD_P]), ALU.mult).then_inc(M.hupd, 1)
        e.wait_ge(M.hupd, j + 1)
        e.wait_ge(M.hst_mm, j + 1)
        V.tensor_tensor(dst[:], K.ht[:], K.ps[:, 6], ALU.add).then_inc(M.hst_read, 1)
        if j == TP // P - 1:
            e.wait_ge(M.Hin, 16)
            V.tensor_copy(K.H[:], K.Hin[:]).then_inc(M.H, 1)
        e.wait_ge(M.y_mm, j + 1)
        wait(e, M.y2, j)
        for u in range(4):
            ins = V.scalar_tensor_tensor(out=K.yt[:, u, :r], in0=K.xc[:, u, a:a + r],
                                         scalar=K.vec[:, V_D + u:V_D + u + 1], in1=K.ps[:, 5, P * u:P * u + r],
                                         op0=ALU.mult, op1=ALU.add)
        ins.then_inc(M.y1, 1)

    def operands(j):
        a, r = TILES[j]
        e.wait_ge(M.x_mm, j + 1)
        wait(e, M.hst_read, j)
        px = K.ps[:r, 2].rearrange("p (h q) -> p h q", h=SSD_H)
        V.tensor_tensor(heads(K.xdt, r), px, K.tk[:r, 8:16].rearrange("p (h o) -> p h o", o=1)
                        .to_broadcast([r, SSD_H, SSD_P]), ALU.mult).then_inc(M.xdt, 1)
        e.wait_ge(M.de1, j + 1)
        M.dve(V.tensor_tensor(K.de[:r, 8:16], K.de[:r, 0:8], K.tk[:r, 8:16], ALU.mult))
        V.tensor_tensor(heads(K.xde, r), px, K.de[:r, 8:16].rearrange("p (h o) -> p h o", o=1)
                        .to_broadcast([r, SSD_H, SSD_P]), ALU.mult).then_inc(M.x_read, 1)
        e.wait_ge(M.eseg, j + 1)
        e.wait_ge(M.cb2_mm, j + 1)
        for u in range(2):
            ins = V.tensor_tensor(K.seg[:r, j % 2, 4 * u:4 * u + 4, :r], K.seg[:r, j % 2, 4 * u:4 * u + 4, :r],
                                  K.ps[:r, CB_BANKS[j % 2], P * u:P * u + r].rearrange("p (o q) -> p o q", o=1)
                                  .to_broadcast([r, 4, r]), ALU.mult)
        ins.then_inc(M.m, 1)

    for j in range(NTT):
        decays(j)
        if j:
            state(j - 1)
        operands(j)
    state(NTT - 1)
    for n in range(2 * NPC):
        a, b = PIECES[n % NPC]
        e.wait_ge(M.yrs, n + 1)
        for u in range(2):
            t = 2 * (n // NPC) + u
            V.scalar_tensor_tensor(out=K.z[:, t, a:b], in0=K.z[:, t, a:b], scalar=K.vec[:, V_SN + t:V_SN + t + 1],
                                   in1=K.n32[:, n % 2, :b - a], op0=ALU.mult, op1=ALU.mult).then_inc(M.ynorm, 1)


def ssd_pool(K, e, M, outs):
    def carried(j):
        a, r = TILES[j]
        e.wait_ge(M.ea, j + 1)
        wait(e, M.h_read, j - 1)
        for u in range(2):
            ins = K.nc.gpsimd.tensor_tensor(K.cea[:, j % 2, 4 * u:4 * u + 4, :r],
                                            K.xc[:, 6 + u, a:a + r].rearrange("p (o q) -> p o q", o=1)
                                            .to_broadcast([P, 4, r]), K.ea[:, j % 2, 4 * u:4 * u + 4, :r], ALU.mult)
        ins.then_inc(M.cea, 1)

    carried(0)
    for j, (a, r) in enumerate(TILES):
        if j + 1 < NTT:
            carried(j + 1)
        e.wait_ge(M.y1, j + 1)
        K.nc.gpsimd.tensor_tensor(K.z[:, :, a:a + r], K.z[:, :, a:a + r], K.yt[:, :, :r], ALU.mult).then_inc(M.y2, 1)
    e.wait_ge(M.hst_read, NTT)
    e.dma_start(outs["ssd"][0], K.Hp[:]).then_inc(M.h_out, 16)
    e.dma_start(outs["ssd"][1], K.Hs[:]).then_inc(M.h_out, 16)


def mixed_tile(K, k):
    return K.z[:, k] if k < 4 else K.gg[:, k - 4] if k < 6 else K.fq[:, k - 6]


MIX_ORDER = (6, 7, 4, 5, 0, 1, 2, 3)


def out_act(K, e, M, follow):
    nc = K.nc
    e.wait_ge(M.proj_mm, IN_START[IN_STEPS])
    e.wait_ge(M.fo, NU)
    e.wait_ge(M.gout, 2 * NPC)
    e.wait_ge(M.h_out, 32)
    e.wait_ge(M.out, 16 * MIX_OUTS)
    for k in MIX_ORDER:
        if k < 4:
            e.wait_ge(M.ynorm, 4 * NPC)
        nc.scalar.copy(K.nh[:, k], mixed_tile(K, k)).then_inc(M.mhi, 1)
    for t in range(OUT_STEPS):
        S = BASE_OUT + t
        if t:
            e.wait_ge(M.out_mm, 2 * NPC * t)
        split_hi(K, e, S + 1, (S + 1) % 2)
        follow_act(K, e, follow, M.out_read, 0, (2 * t, 2 * t + 1))


def out_dve(K, e, M):
    V = K.nc.vector
    for n, k in enumerate(MIX_ORDER):
        e.wait_ge(M.mhi, n + 1)
        V.tensor_tensor(K.nl[:, k], mixed_tile(K, k), K.nh[:, k].bitcast(F32), ALU.subtract).then_inc(M.mlo, 1)
    for t in range(OUT_STEPS):
        S = BASE_OUT + t
        split_lo(K, e, S + 1, (S + 1) % 2)
        for m in range(2):
            d = 2 * t + m
            e.wait_ge(M.x_back[t], 16)
            for j, (a, b) in enumerate(PIECES):
                n = NPC * d + j
                e.wait_ge(M.out_mm, n + 1)
                V.tensor_tensor(K.x[:, d, a:b], K.ps[:, n % 4, :b - a], K.x[:, d, a:b], ALU.add)\
                    .then_inc(M.out_read, 1)


def out_pe(K, e, M):
    e.wait_ge(M.mlo, KT)
    e.wait_ge(M.yln, 2 * NPC)
    for t in range(OUT_STEPS):
        S = BASE_OUT + t
        e.wait_ge(K.w_lo, 2 * (S + 1))
        whi = K.whi[:, S % 2].rearrange("p (m k n) -> p m k n", m=2, k=KT)
        wlo = K.wlo[:, S % 2].rearrange("p (m k n) -> p m k n", m=2, k=KT)
        for m in range(2):
            for j, (a, b) in enumerate(PIECES):
                n = NPC * (2 * t + m) + j
                wait(e, M.out_read, n - 3)
                for k in range(KT):
                    mm = three(K, K.ps[:, n % 4, :b - a], whi[:, m, k], wlo[:, m, k],
                               K.nh[:, k, a:b], K.nl[:, k, a:b], k == 0, k == KT - 1)
                mm.then_inc(M.out_mm, 1)


class NormSems:

    def __init__(self, sem, tag):
        self.sq = sem(tag + "sq")
        self.added = sem(tag + "added")
        self.sum_mm = sem(tag + "sum_mm")
        self.rstd = sem(tag + "rstd")
        self.n32 = sem(tag + "n32")
        self.hi = sem(tag + "hi")
        self.lo = sem(tag + "lo")
        self.lo_odd = sem(tag + "lo_odd")


class FfnSems:

    def __init__(self, sem, tag):
        self.sq = sem(tag + "sq")
        self.added = sem(tag + "added")
        self.sum_mm = sem(tag + "sum_mm")
        self.rstd = sem(tag + "rstd")
        self.n32 = sem(tag + "n32")
        self.hi = sem(tag + "hi")
        self.lo = sem(tag + "lo")
        self.lo_odd = sem(tag + "lo_odd")
        self.gate_mm = sem(tag + "gate_mm")
        self.up_mm = sem(tag + "up_mm")
        self.down_mm = sem(tag + "down_mm")
        self.silu = sem(tag + "silu")
        self.h32 = sem(tag + "h32")
        self.hhi = sem(tag + "hhi")
        self.hlo = sem(tag + "hlo")
        self.x_upd = sem(tag + "x_upd")


class SoftplusSems:

    def __init__(self, sem, tag):
        self.absv = sem(tag + "absv")
        self.e = sem(tag + "e")
        self.u = sem(tag + "u")
        self.ln = sem(tag + "ln")


class MixSems:

    def __init__(self, sem, tag):
        self.proj_mm = sem(tag + "proj_mm")
        self.proj_read = sem(tag + "proj_read")
        self.chain = sem(tag + "chain")
        self.x_out = sem(tag + "x_out")
        self.cache = sem(tag + "cache")
        self.out = sem(tag + "out")
        self.kout = sem(tag + "kout")
        self.h_out = sem(tag + "h_out")
        self.Sin = sem(tag + "Sin")
        self.Hin = sem(tag + "Hin")
        self.cprev = sem(tag + "cprev")
        self.fsq = sem(tag + "fsq")
        self.fss = sem(tag + "fss")
        self.fln = sem(tag + "fln")
        self.frs = sem(tag + "frs")
        self.fqk = sem(tag + "fqk")
        self.logf = sem(tag + "logf")
        self.cum = sem(tag + "cum")
        self.cb_mm = sem(tag + "cb_mm")
        self.cb = sem(tag + "cb")
        self.s_mm = sem(tag + "s_mm")
        self.smin = sem(tag + "smin")
        self.p_exp = sem(tag + "p_exp")
        self.rinv = sem(tag + "rinv")
        self.p_scaled = sem(tag + "p_scaled")
        self.pt_mm = sem(tag + "pt_mm")
        self.pt_a = sem(tag + "pt_a")
        self.pt_v = sem(tag + "pt_v")
        self.o_mm = sem(tag + "o_mm")
        self.fo = sem(tag + "fo")
        self.g_mm = sem(tag + "g_mm")
        self.bcum = sem(tag + "bcum")
        self.eb = sem(tag + "eb")
        self.enb = sem(tag + "enb")
        self.bdiff = sem(tag + "bdiff")
        self.ebd = sem(tag + "ebd")
        self.kend = sem(tag + "kend")
        self.gqk = sem(tag + "gqk")
        self.kt_mm = sem(tag + "kt_mm")
        self.kt_read = sem(tag + "kt_read")
        self.att_mm = sem(tag + "att_mm")
        self.att = sem(tag + "att")
        self.S = sem(tag + "S")
        self.st_mm = sem(tag + "st_mm")
        self.st_read = sem(tag + "st_read")
        self.S_end = sem(tag + "S_end")
        self.go_mm = sem(tag + "go_mm")
        self.go_read = sem(tag + "go_read")
        self.gsq = sem(tag + "gsq")
        self.gss = sem(tag + "gss")
        self.gln = sem(tag + "gln")
        self.grs = sem(tag + "grs")
        self.gnorm = sem(tag + "gnorm")
        self.gout = sem(tag + "gout")
        self.pad = sem(tag + "pad")
        self.prev = sem(tag + "prev")
        self.raw_tail = sem(tag + "raw_tail")
        self.tail = sem(tag + "tail")
        self.conv = sem(tag + "conv")
        self.xc = sem(tag + "xc")
        self.ealog = sem(tag + "ealog")
        self.acum = sem(tag + "acum")
        self.H = sem(tag + "H")
        self.a_mm = sem(tag + "a_mm")
        self.x_mm = sem(tag + "x_mm")
        self.b_mm = sem(tag + "b_mm")
        self.cb2_mm = sem(tag + "cb2_mm")
        self.h_read = sem(tag + "h_read")
        self.y_mm = sem(tag + "y_mm")
        self.hst_mm = sem(tag + "hst_mm")
        self.seg = sem(tag + "seg")
        self.ea = sem(tag + "ea")
        self.de0 = sem(tag + "de0")
        self.de1 = sem(tag + "de1")
        self.sm_read = sem(tag + "sm_read")
        self.cea = sem(tag + "cea")
        self.xdt = sem(tag + "xdt")
        self.x_read = sem(tag + "x_read")
        self.b_read = sem(tag + "b_read")
        self.eseg = sem(tag + "eseg")
        self.m = sem(tag + "m")
        self.hupd = sem(tag + "hupd")
        self.hst_read = sem(tag + "hst_read")
        self.y1 = sem(tag + "y1")
        self.y2 = sem(tag + "y2")
        self.ysq = sem(tag + "ysq")
        self.yss = sem(tag + "yss")
        self.yln = sem(tag + "yln")
        self.yrs = sem(tag + "yrs")
        self.ynorm = sem(tag + "ynorm")
        self.mhi = sem(tag + "mhi")
        self.mlo = sem(tag + "mlo")
        self.out_mm = sem(tag + "out_mm")
        self.out_read = sem(tag + "out_read")


class Core:
    pass


MIX_OUTS = 2 + 1 + 2 * GLA_H + 1


def second(u):
    return sum(len(fox_groups(j)) > 1 for _, j in FOX_UNITS[:u])


def hybrid_layer(nc, i, o):
    with ExitStack() as ctx:
        K = Core()
        K.nc, K.second = nc, second

        def sb(name, shape, dt=F32, scope=ctx):
            return scope.enter_context(nc.sbuf_tensor("sb_" + name, shape, dt))

        def sem(name):
            return ctx.enter_context(nc.semaphore(name))

        ps = ctx.enter_context(nc.psum_tensor("ps", [P, 8, 512], F32))
        K.ps = ps
        K.psf = ps[:].rearrange("p b n -> p (b n)")

        with ExitStack() as r:
            K.cea = sb("cea", [P, 2, SSD_H, P], scope=r)
            K.ea = sb("ea", [P, 2, SSD_H, P], scope=r)
        K.nh = sb("nh", [P, KT, T], F32R)
        K.wraw = sb("wraw", [P, STEP])
        K.whi = sb("whi", [P, 2, STEP], F32R)
        K.wlo = sb("wlo", [P, 2, STEP], F32R)
        K.const = sb("const", [P, NCONST])
        K.vec = sb("vec", [P, NVEC])
        K.eps = sb("eps", [P, 1])
        K.eal = sb("eal", [P, 1])
        K.sq = sb("sq", [P, 2, W])
        K.n32 = sb("n32", [P, 2, W])
        K.lnv = sb("lnv", [P, W])
        c = K.const
        K.ident, K.ones, K.b64 = c[:, C_ID:C_ID + P], c[:, C_ONE:C_ONE + P], c[:, C_B64:C_B64 + P]
        K.mqk, K.msl = c[:, C_MQK:C_MQK + P], c[:, C_MSL:C_MSL + P]
        K.gmask = c[:, C_GM:C_GM + P].bitcast(I32)
        K.bmask = c[:, C_BM:C_BM + 256]

        with ExitStack() as r:
            K.pre = sb("pre", [P, 2, T], scope=r)
        with ExitStack() as r:
            K.seg = sb("seg", [P, 2, SSD_H, P], scope=r)
            K.xdt = sb("xdt", [P, 512], scope=r)
            K.xde = sb("xde", [P, 512], scope=r)
            K.btok = sb("btok", [P, 256], scope=r)
            K.H = sb("H", [P, 512], scope=r)
            K.Hp = sb("Hp", [P, 512], scope=r)
            K.Hs = sb("Hs", [P, 512], scope=r)
            K.Hin = sb("Hin", [P, 512], scope=r)
            K.ht = sb("ht", [P, 512], scope=r)
            K.yt = sb("yt", [P, 4, P], scope=r)
            K.adt = sb("adt", [P, T], scope=r)
            K.tk = sb("tk", [P, 16], scope=r)
            K.de = sb("de", [P, 16], scope=r)
        K.nl = sb("nl", [P, KT, T], F32R)

        with ExitStack() as r:
            K.cb = sb("cb", [P, 2, CUM], scope=r)
            K.pr = sb("pr", [P, 3, 1024], scope=r)
            K.kc = sb("kc", [P, 2, PAST], scope=r)
            K.vc = sb("vc", [P, PAST // P, 256], scope=r)
            flat = K.pr[:].rearrange("p s n -> p (s n)")
            K.t1, K.t2, K.lfc = flat[:, 0:T], flat[:, T:2 * T], flat[:, 3 * 1024 - PAST:]
        with ExitStack() as r:
            K.gd = sb("gd", [P, T], scope=r)
            K.ga = sb("ga", [P, T], scope=r)
            K.gb = sb("gb", [P, T], scope=r)
            K.ge = sb("ge", [P, T], scope=r)
            K.go = sb("go", [P, 2, T], scope=r)
            K.kt = sb("kt", [P, NTT, P], scope=r)
            K.attn = sb("attn", [P, 2, GLA_H, P], scope=r)
        with ExitStack() as r:
            K.xc = sb("xc", [P, 8, T], scope=r)
        K.x = sb("x", [P, KT, T])

        with ExitStack() as r:
            sb("norm_hh0", [P, 2, T], scope=r)
            K.rms = sb("rms", [P, T], scope=r)
            sb("norm_gap", [P, 2, T], scope=r)
            K.sq_first = sb("sq_first", [P, 4, W], scope=r)
        with ExitStack() as r:
            sb("norm_low", [P, 8 * T - 4 * W], scope=r)
            K.nrm = sb("nrm", [P, 4, W], scope=r)
            K.sqs = sb("sqs", [P, 4, W], scope=r)
        with ExitStack() as r:
            K.hh = sb("hh", [P, 2, 2, T], F32R, scope=r)
            K.hl = sb("hl", [P, 2, 2, T], F32R, scope=r)
            K.sg = sb("sg", [P, 2, W], scope=r)
            K.h32 = sb("h32", [P, 2, W], scope=r)
        K.fq = sb("fq", [P, 2, T])
        K.small = sb("small", [P, T])
        with ExitStack() as r:
            K.pt = sb("pt", [P, 2, 8, P], scope=r)
        K.gg = sb("gg", [P, 2, T])
        with ExitStack() as r:
            K.gk = sb("gk", [P, T], scope=r)
            K.fk = sb("fk", [P, 2, T], scope=r)
            K.fv = sb("fv", [P, NTT, 256], scope=r)
            K.cum = sb("cum", [P, CUM], scope=r)
            K.mn = sb("mn", [P, 3], scope=r)
            K.rs = sb("rs", [P, 3], scope=r)
            K.ri = sb("ri", [P, 3], scope=r)
        with ExitStack() as r:
            sb("gk_again", [P, T], scope=r)
            K.gq = sb("gq", [P, T], scope=r)
            K.gv = sb("gv", [P, NTT, 256], scope=r)
            K.S = sb("S", [P, 4, 256], scope=r)
            K.gst = sb("gst", [P, 256], scope=r)
            K.Sin = sb("S_in", [P, 256], scope=r)
            K.Sp = sb("S_prompt", [P, 256], scope=r)
            K.Ss = sb("S_decoder", [P, 256], scope=r)
            K.glast = sb("glast", [P, GCH], scope=r)
        with ExitStack() as r:
            K.raw = sb("raw", [P, 2, T + 6], scope=r)
            K.acc = sb("acc", [P, 2, T + 3], scope=r)
            K.cprev = sb("cprev", [P, 8, 3], scope=r)
            K.ctail = sb("ctail", [P, 8, 2, 3], scope=r)
        with ExitStack() as r:
            K.z = sb("z", [P, 4, T], scope=r)

        K.w_loaded, K.w_hi, K.w_lo = sem("w_loaded"), sem("w_hi"), sem("w_lo")
        K.x_in = [sem(f"x_in{c}") for c in range(NPC)]
        K.ones_in, K.consts_in, K.epsw, y_out = sem("ones_in"), sem("consts_in"), sem("eps_set"), sem("y_out")
        F1, F2 = FfnSems(sem, "ffn1_"), FfnSems(sem, "ffn2_")
        M = MixSems(sem, "mix_")
        M.norm = NormSems(sem, "mixnorm_")
        M.sp, M.gsp = SoftplusSems(sem, "small_"), SoftplusSems(sem, "gla_")
        M.x_back = [sem(f"x_back{t}") for t in range(OUT_STEPS)]

        act_chain = sem("act_chain")

        block = ctx.enter_context(nc.Block())

        @block.sync
        def _(sp):
            x = i["x"].rearrange("(k p) t -> p k t", p=P)
            sp.dma_start(K.x[:, :, :W], x[:, :, :W]).then_inc(K.x_in[0], 16)
            sp.dma_start(K.ones, i["const"][:, C_ONE:C_ONE + P]).then_inc(K.ones_in, 16)
            sp.dma_start(K.vec[:], i["vec"]).then_inc(K.ones_in, 16)
            sp.dma_start(K.wraw[:], i["weights"][0]).then_inc(K.w_loaded, 16)
            for c, (a, b) in list(enumerate(PIECES))[1:]:
                sp.dma_start(K.x[:, :, a:b], x[:, :, a:b]).then_inc(K.x_in[c], 16)
            for cols in (slice(0, C_ONE), slice(C_ONE + P, NCONST)):
                sp.dma_start(K.const[:, cols], i["const"][:, cols]).then_inc(K.consts_in, 16)
            with sp.Fori(1, NSTEPS) as s:
                sp.wait_ge(K.w_lo, s * 2)
                sp.dma_start(K.wraw[:], i["weights"][s]).then_inc(K.w_loaded, 16)
            for d in range(KT):
                sp.wait_ge(F2.x_upd, DN * 10 + NPC * (d + 1))
                sp.dma_start(o["y"][d * P:(d + 1) * P], K.x[:, d]).then_inc(y_out, 16)
            sp.wait_ge(y_out, 16 * KT)

        @block.tensor
        def _(e):
            e.wait_ge(K.ones_in, 32)
            first_sums_pe(K, e, F1)
            ffn_pe(K, e, F1, BASE1)
            follow_pe(K, e, M.norm)
            e.wait_ge(K.consts_in, 32)
            for t in range(IN_STEPS):
                if t == FOX_AT:
                    fox_pe(K, e, M)
                if t == GLA_AT:
                    gla_pe(K, e, M)
                proj_pe(K, e, M, t)
            ssd_pe(K, e, M)
            out_pe(K, e, M)
            follow_pe(K, e, F2)
            ffn_pe(K, e, F2, BASE2)

        @block.scalar
        def _(e):
            K.act = Chain(e, act_chain)
            e.wait_ge(K.epsw, 1)

            def first_split(e, N):
                if N is F2:
                    e.wait_ge(M.out_mm, NPC * KT)
            K.before_split_act = first_split

            def first_split_proj(e, M):
                e.wait_ge(F1.down_mm, DN * 11)
            K.before_split_proj = first_split_proj

            nc.scalar.preload_act_table_set(LOG_EXP)
            norm_act(K, e, F1, SUMS_FIRST)
            ffn_act(K, e, F1, BASE1, follow=M.norm)
            norm_act(K, e, M.norm, SUMS_LATER)
            e.wait_ge(K.consts_in, 32)
            for t in range(IN_STEPS):
                if t == FOX_AT:
                    fox_act(K, e, M)
                if t == GLA_AT:
                    gla_act(K, e, M)
                proj_act(K, e, M, t)
            ssd_act(K, e, M)
            out_act(K, e, M, follow=F2)
            norm_act(K, e, F2, SUMS_LATER)
            ffn_act(K, e, F2, BASE2)

        @block.vector
        def _(e):
            M.dve = Chain(e, M.chain)
            nc.vector.memset(K.eps[:], EPS).then_inc(K.epsw, 1)
            split_lo(K, e, 0, 0)
            e.wait_ge(K.ones_in, 32)
            norm_dve(K, e, F1, V_N1)
            ffn_dve(K, e, F1, BASE1)
            norm_dve(K, e, M.norm, V_NM)
            e.wait_ge(K.consts_in, 32)
            for t in range(IN_STEPS):
                if t == FOX_AT:
                    fox_dve(K, e, M)
                if t == GLA_AT:
                    gla_dve(K, e, M)
                split_lo(K, e, BASE_IN + t + 1, (BASE_IN + t + 1) % 2)
                if t >= CONV_AT and IN_PLAN[t][0][0] == "x":
                    conv_dve(K, e, M, t)
            ssd_dve(K, e, M)
            out_dve(K, e, M)
            norm_dve(K, e, F2, V_N2)
            ffn_dve(K, e, F2, BASE2)

        @block.gpsimd
        def _(e):
            norm_pool(K, e, F1)
            follow_pool(K, e, M.norm)
            norm_pool(K, e, M.norm)
            e.wait_ge(F1.x_upd, DN * 11)
            e.dma_start(o["x_kept"], K.x[:]).then_inc(M.x_out, 16)
            e.wait_ge(M.x_out, 16)
            e.wait_ge(M.norm.n32, KT * NPC)
            e.dma_start(K.kc[:], i["kc"].rearrange("(t p) s -> p t s", p=P)).then_inc(M.cache, 16)
            e.dma_start(K.vc[:], i["vc"].rearrange("(t p) n -> p t n", p=P)).then_inc(M.cache, 16)
            e.dma_start(K.lfc[SMALL_FF:SMALL_FF + FOX_H], i["lfc"]).then_inc(M.cache, 16)
            fox_pool(K, e, M, o)
            e.wait_ge(M.fo, NU)
            e.wait_ge(M.kout, 16)
            nc.gpsimd.memset(K.Sin[:], 0.0).then_inc(M.pad, 1)
            e.wait_ge(M.pad, 1)
            for h in range(GLA_H):
                r = slice(GLA_K * h, GLA_K * h + GLA_K)
                e.dma_start(K.Sin[r, 64 * h:64 * h + 64], i["gla"][r]).then_inc(M.Sin, 16)
            gla_pool(K, e, M, o)
            e.wait_ge(M.go_mm, NTT)
            e.dma_start(K.cprev[:], i["cprev"].rearrange("(u p) s -> p u s", p=P)).then_inc(M.cprev, 16)
            e.wait_ge(M.cprev, 16)
            conv_pool(K, e, M, o["tail"])
            e.wait_ge(M.proj_mm, IN_START[IN_STEPS])
            e.dma_start(K.Hin[:], i["ssd"]).then_inc(M.Hin, 16)
            ssd_pool(K, e, M, o)
            e.wait_ge(M.y2, NTT)
            for t in range(OUT_STEPS):
                e.dma_start(K.x[:, 2 * t:2 * t + 2], o["x_kept"][:, 2 * t:2 * t + 2]).then_inc(M.x_back[t], 16)
            e.wait_ge(M.out, 16 * MIX_OUTS)
            e.wait_ge(M.h_out, 32)
            follow_pool(K, e, F2)
            norm_pool(K, e, F2)


def shape_constants():
    c = np.zeros((P, NCONST), np.float32)
    r = np.arange(P)
    c[:, C_ID:C_ID + P] = np.eye(P)
    c[:, C_ONE:C_ONE + P] = 1.0
    c[:, C_B64:C_B64 + P] = r[:, None] // 64 == r[None] // 64
    c[:, C_MQK:C_MQK + P] = np.where(r[None] <= r[:, None], 0.0, -BIG)
    c[:, C_MSL:C_MSL + P] = np.where(r[:, None] <= r[None], 0.0, -BIG)
    c[:, C_GM:C_GM + P] = (r[:, None] <= r[None]) & (r[:, None] // GLA_L == r[None] // GLA_L)
    c[:, C_BM:C_BM + 256] = r[:, None] // GLA_K == np.arange(256)[None] // GLA_V
    for h in range(SSD_H):
        c[SMALL_DT + h, C_SEL + h * P:C_SEL + (h + 1) * P] = 1.0
    for h in range(FOX_H):
        c[SMALL_FF + h, C_SEL + h * P:C_SEL + (h + 1) * P] = -8.0
    return c


def kernel(**inputs):
    import concourse.bacc as bacc
    from concourse.bass_utils import run_bass_kernel_spmd

    v = {n: np.asarray(a) for n, a in inputs.items()}
    f32 = np.float32

    def column_tile(w):
        return w.reshape(KT, P, P).transpose(1, 0, 2).reshape(P, D)

    def swiglu(gate, up, down):
        steps = []
        for kind, c in (FFN_HEAD + [(k, c + (4 if k == "up" else 2) * it) for it in range(FFN_LOOPS)
                                    for k, c in FFN_BODY] + FFN_TAIL):
            if kind == "up":
                cols = slice(P * c, P * c + P)
                steps.append(np.concatenate([column_tile(gate[:, cols]), column_tile(up[:, cols])], 1))
            else:
                steps.append(down[2 * P * c:2 * P * (c + 1)].reshape(2, P, D).transpose(1, 0, 2).reshape(P, STEP))
        return steps

    sizes = dict(z=512, x=1024, dt=8, gq=128, gk=128, gv=256, gg=256, gr=16, fq=256, fk=256, fv=256, ff=4)
    w_in, off, cols = v["w_in"][0], 0, {}
    for n, s in sizes.items():
        cols[n] = w_in[:, off:off + s]
        off += s
    small = np.zeros((D, P), f32)
    small[:, 0:GLA_R] = cols["gr"]
    small[:, SMALL_DT:SMALL_DT + SSD_H] = cols["dt"]
    small[:, SMALL_FF:SMALL_FF + FOX_H] = cols["ff"]

    def in_tile(name):
        if name in ("small", "gq", "gk"):
            return column_tile(small if name == "small" else cols[name])
        u = int(name[-1])
        return column_tile(cols[name.rstrip("0123456789")][:, P * u:P * u + P])

    steps = swiglu(v["w1_gate"][0], v["w1_up"][0], v["w1_down"][0])
    for s in IN_PLAN:
        if isinstance(s, str):
            steps.append(cols[s].reshape(KT, P, 256).transpose(1, 0, 2).reshape(P, STEP))
        else:
            tiles = [in_tile(n) for n in s] + [np.zeros((P, D), f32)] * (2 - len(s))
            steps.append(np.concatenate(tiles, 1))
    w_out = v["w_out"][0]
    for t in range(OUT_STEPS):
        steps.append(np.concatenate([column_tile(w_out[:, P * d:P * d + P]) for d in (2 * t, 2 * t + 1)], 1))
    steps += swiglu(v["w2_gate"][0], v["w2_up"][0], v["w2_down"][0])

    tiled = lambda a: a.reshape(-1, P).T
    vec = np.zeros((P, NVEC), f32)
    vec[:, V_N1:V_N1 + 8] = tiled(v["norm_ffn1"][0])
    vec[:, V_NM:V_NM + 8] = tiled(v["norm_mix"][0])
    vec[:, V_N2:V_N2 + 8] = tiled(v["norm_ffn2"][0])
    vec[:, V_CW:V_CW + 32] = v["ssd_conv_w"][0].reshape(4, 8, P).transpose(2, 1, 0).reshape(P, 32)
    vec[:, V_CB:V_CB + 8] = tiled(v["ssd_conv_b"][0])
    vec[SMALL_DT:SMALL_DT + SSD_H, V_SB] = v["ssd_dt_bias"][0]
    vec[SMALL_FF:SMALL_FF + FOX_H, V_SB] = v["fox_f_bias"][0]
    vec[SMALL_DT:SMALL_DT + SSD_H, V_AL] = v["ssd_a_log"][0]
    vec[:, V_D:V_D + 4] = tiled(np.repeat(v["ssd_d"][0], SSD_P))
    vec[:, V_SN:V_SN + 4] = tiled(v["ssd_norm"][0])
    vec[:, V_GB] = v["gla_b_gate"][0]
    vec[:, V_GN] = np.tile(v["gla_norm"][0], 2)
    vec[:, V_QN] = np.tile(v["fox_q_norm"][0], 2)
    vec[:, V_KN] = np.tile(v["fox_k_norm"][0], 2)
    const = shape_constants()
    const[:GLA_R, C_SEL:C_SEL + P] = v["gla_w_gate"][0]

    arrays = dict(
        x=np.concatenate([v["x_prompt"][0], v["x_sample"][0]], 0).T,
        weights=np.stack(steps),
        const=const, vec=vec,
        kc=v["cache_fox_k"][0, 0].reshape(PAST, 256).T,
        vc=v["cache_fox_v"][0, 0].reshape(PAST, 256),
        lfc=v["cache_fox_logf"][0, 0].T,
        gla=v["state_gla"][0, 0].reshape(P, GLA_V),
        cprev=v["state_ssd_conv"][0, 0].T,
        ssd=v["state_ssd"][0, 0].transpose(2, 0, 1).reshape(SSD_N, 512),
    )
    arrays = {n: np.ascontiguousarray(a, f32) for n, a in arrays.items()}
    out_shapes = dict(y=(D, T), tail=(P, 8, 2, 3), ssd=(2, P, 512), gla=(2, P, GLA_V), k=(P, 2, T),
                      v=(T, 256), logf=(FOX_H, T))

    nc = bacc.Bacc("TRN2", target_bir_lowering=False, num_devices=1)
    ins = {n: nc.dram_tensor(n, a.shape, F32, kind="ExternalInput").ap() for n, a in arrays.items()}
    outs = {n: nc.dram_tensor("out_" + n, s, F32, kind="ExternalOutput").ap() for n, s in out_shapes.items()}
    outs["x_kept"] = nc.dram_tensor("x_kept", (P, KT, T), F32, kind="Internal").ap()
    outs["v"] = [outs["v"][:TP].rearrange("(j p) n -> p j n", p=P),
                 outs["v"][TP:].rearrange("(j p) n -> p j n", p=TS)]
    hybrid_layer(nc, ins, outs)
    got = run_bass_kernel_spmd(nc, [arrays], core_ids=[0]).results[0]
    g = {n: got["out_" + n] for n in out_shapes}

    def rows(a, b):
        k = g["k"].transpose(2, 1, 0).reshape(T, FOX_H, FOX_D)[a:b]
        return (g["y"].T[a:b][None], k[None, None], g["v"].reshape(T, FOX_H, FOX_D)[a:b][None, None],
                g["logf"].T[a:b][None, None])

    def states(j):
        conv = g["tail"][:, :, j].transpose(2, 1, 0).reshape(1, 1, 3, 1024)
        ssd = g["ssd"][j].reshape(SSD_N, SSD_H, SSD_P).transpose(1, 2, 0)[None, None]
        return conv, ssd, g["gla"][j].reshape(1, 1, GLA_H, GLA_K, GLA_V)

    (yp, kp, vp, fp), (ys, ks, vs, fs) = rows(0, TP), rows(TP, T)
    return (yp, ys, *states(0), kp, vp, fp, *states(1), ks, vs, fs)
```

```python
from contextlib import ExitStack

import numpy as np

import concourse.bass as bass
from concourse import mybir

ALU = mybir.AluOpType
ACT = mybir.ActivationFunctionType
F32 = mybir.dt.float32
F32R = mybir.dt.float32r
I32 = mybir.dt.int32

P = 128
D = 1024
KT = D // P
TP, TS = 1024, 64
T = TP + TS
PIECES = ((0, 364), (364, 726), (726, T))
NPC = len(PIECES)
W = 364
FF = 2816
FT = FF // P
PAST = 512
EPS = 1e-6
BIG = 1e30
LOG_EXP = "natural_log_exp_and_others"

SSD_H, SSD_P, SSD_N = 8, 64, 128
GLA_H, GLA_K, GLA_V, GLA_R, GLA_TAU = 4, 32, 64, 16, 16.0
FOX_H, FOX_D = 4, 64
TILES = [(j * P, min(P, T - j * P)) for j in range((T + P - 1) // P)]
NTT = len(TILES)
SMALL_DT, SMALL_FF = 32, 64

STEP = 2 * D
FFN_STEPS = FT + FT // 2
IN_STEPS = 13
OUT_STEPS = 4
BASE1 = 0
BASE_IN = FFN_STEPS
BASE_OUT = BASE_IN + IN_STEPS
BASE2 = BASE_OUT + OUT_STEPS
NSTEPS = BASE2 + FFN_STEPS

IN_PLAN = [("fq0", "fq1"), ("fk0", "fk1"), ("small", "gk"), "fv", ("gq",), "gv", ("gg0", "gg1"),
           ("x0", "x1"), ("x2", "x3"), ("x4", "x5"), ("x6", "x7"), ("z0", "z1"), ("z2", "z3")]
IN_PIECES = [NTT if isinstance(s, str) else NPC * len(s) for s in IN_PLAN]
IN_START = [sum(IN_PIECES[:t]) for t in range(IN_STEPS + 1)]
FOX_AT, GLA_AT, CONV_AT = 4, 7, 7
FOX_SMALL_AT, FOX_NORM_AT, GLA_GATE_AT = 2, 3, 5

C_ID, C_ONE, C_B64, C_MSL, C_MQK, C_GM, C_BM, C_SEL = 0, 128, 256, 384, 512, 640, 768, 1024
NCONST = C_SEL + SSD_H * P
V_N1, V_NM, V_N2, V_CW, V_CB, V_SB, V_AL, V_D, V_SN, V_GB, V_GN, V_QN, V_KN = (
    0, 8, 16, 24, 56, 64, 65, 66, 70, 74, 75, 76, 77)
NVEC = 78
CUM = TP + PAST + TS


def at(i, per_body, c):
    return c if i is None else i * per_body + c


def wait(e, sem, value):
    if not isinstance(value, int) or value > 0:
        e.wait_ge(sem, value)


class Chain:

    def __init__(self, e, sem):
        self.e, self.sem, self.n = e, sem, 0

    def __call__(self, ins):
        self.n += 1
        ins.then_inc(self.sem, 1)
        self.e.wait_ge(self.sem, self.n)


def split_hi(K, e, S, parity):
    e.wait_ge(K.w_loaded, 16 * (S + 1))
    K.nc.scalar.copy(K.whi[:, parity], K.wraw[:]).then_inc(K.w_hi, 1)


def split_lo(K, e, S, parity, halves=(0, 1)):
    for h in halves:
        c = slice(h * D, h * D + D)
        if h == 0:
            e.wait_ge(K.w_hi, S + 1)
        K.nc.vector.tensor_tensor(K.wlo[:, parity, c], K.wraw[:, c], K.whi[:, parity, c].bitcast(F32),
                                  ALU.subtract).then_inc(K.w_lo, 1)


def three(K, out, whi, wlo, xhi, xlo, first, last, token_major=False):
    mm = None
    for n, (w, x) in enumerate(((whi, xhi), (whi, xlo), (wlo, xhi))):
        a, b = (x, w) if token_major else (w, x)
        mm = K.nc.tensor.matmul(out, a, b, start=first and n == 0, stop=last and n == 2)
    return mm


SUMS_FIRST, SUMS_LATER = KT, 1


def follow_act(K, e, N, updated, base, tiles=range(KT), tile_waits=False):
    for d in tiles:
        for j, (a, b) in enumerate(PIECES):
            o = NPC * d + j
            e.wait_ge(updated, base + (NPC * (d // 2 * 2 + 2) if tile_waits else o + 1))
            wait(e, N.added, o - 2 * NPC)
            dst = K.rms[:, a:b] if d == 0 else K.sqs[:, (o - NPC) % 4, :b - a]
            K.nc.scalar.activation(dst, K.x[:, d, a:b], ACT.Square).then_inc(N.sq, 1)


def follow_pool(K, e, N):
    for d in range(1, KT):
        for j, (a, b) in enumerate(PIECES):
            o = NPC * d + j
            e.wait_ge(N.sq, o + 1)
            wait(e, N.added, o - 2 * NPC + 1)
            K.nc.gpsimd.tensor_tensor(K.rms[:, a:b], K.rms[:, a:b], K.sqs[:, (o - NPC) % 4, :b - a],
                                      ALU.add).then_inc(N.added, 1)


def follow_pe(K, e, N):
    for c, (a, b) in enumerate(PIECES):
        e.wait_ge(N.added, NPC * (KT - 2) + c + 1)
        K.nc.tensor.matmul(K.ps[:, 4 + c, :b - a], K.ones, K.rms[:, a:b], start=True,
                           stop=True).then_inc(N.sum_mm, 1)


def first_sum_pe(K, e, N, c):
    a, b = PIECES[c]
    for k in range(KT):
        n = KT * c + k
        e.wait_ge(N.sq, n + 1)
        K.nc.tensor.matmul(K.ps[:, 4 + c, :b - a], K.ones, K.sq_first[:, n % 4, :b - a],
                           start=k == 0, stop=k == KT - 1).then_inc(N.sum_mm, 1)


def norm_act(K, e, N, sums):
    nc = K.nc

    def square(c, k):
        a, b = PIECES[c]
        n = KT * c + k
        if k == 0:
            e.wait_ge(K.x_in[c], 16)
        wait(e, N.sum_mm, n - 3)
        nc.scalar.activation(K.sq_first[:, n % 4, :b - a], K.x[:, k, a:b], ACT.Square).then_inc(N.sq, 1)

    def rms(c):
        a, b = PIECES[c]
        e.wait_ge(N.sum_mm, sums * (c + 1))
        K.act(nc.scalar.activation(K.rms[:, a:b], K.ps[:, 4 + c, :b - a], ACT.Ln, bias=K.eps[:, 0:1],
                                   scale=1.0 / D))
        nc.scalar.activation(K.rms[:, a:b], K.rms[:, a:b], ACT.Exp, scale=-0.5).then_inc(N.rstd, 1)

    if sums == SUMS_FIRST:
        for k in range(KT):
            square(0, k)
        split_hi(K, e, 0, 0)
    rms(0)
    for c, (a, b) in enumerate(PIECES):
        for k in range(KT):
            n = KT * c + k
            if sums == SUMS_FIRST and c + 1 < NPC and k < KT // 2:
                square(c + 1, 2 * k)
                square(c + 1, 2 * k + 1)
            e.wait_ge(N.n32, n + 1)
            nc.scalar.copy(K.nh[:, k, a:b], K.nrm[:, n % 4, :b - a]).then_inc(N.hi, 1)
            if c + 1 < NPC and k == (5 if sums == SUMS_FIRST else 3):
                rms(c + 1)


def norm_lo(K, e, eng, N, n, done):
    c, k = divmod(n, KT)
    a, b = PIECES[c]
    e.wait_ge(N.hi, n + 1)
    eng.tensor_tensor(K.nl[:, k, a:b], K.nrm[:, n % 4, :b - a], K.nh[:, k, a:b].bitcast(F32),
                      ALU.subtract).then_inc(done, 1)


def norm_dve(K, e, N, gain):
    for c, (a, b) in enumerate(PIECES):
        e.wait_ge(N.rstd, c + 1)
        for k in range(KT):
            n = KT * c + k
            if k % 2:
                wait(e, N.lo_odd, (n - 3) // 2)
            else:
                wait(e, N.lo, n // 2 - 1)
            K.nc.vector.scalar_tensor_tensor(out=K.nrm[:, n % 4, :b - a], in0=K.x[:, k, a:b],
                                             scalar=K.vec[:, gain + k:gain + k + 1],
                                             in1=K.rms[:, a:b], op0=ALU.mult,
                                             op1=ALU.mult).then_inc(N.n32, 1)
            if k % 2:
                norm_lo(K, e, K.nc.vector, N, n - 1, N.lo)


def norm_pool(K, e, N):
    for n in range(1, NPC * KT, 2):
        norm_lo(K, e, K.nc.gpsimd, N, n, N.lo_odd)


def wait_normed(e, N, j, k):
    n = KT * j + k
    e.wait_ge(N.lo_odd if k % 2 else N.lo, n // 2 + 1)


FFN_HEAD = [("up", 0), ("up", 1), ("up", 2), ("up", 3), ("down", 0)]
FFN_BODY = [("up", 4), ("up", 5), ("down", 1), ("up", 6), ("up", 7), ("down", 2)]
FFN_TAIL = [("up", 20), ("up", 21), ("down", 9), ("down", 10)]
FFN_LOOPS = 4
DN = KT * NPC


def ffn_steps(e, run):
    prev = None
    n = 0
    for kind, c in FFN_HEAD:
        run(None, n, kind, c, prev)
        prev = (kind, c)
        n += 1
    with e.Fori(0, FFN_LOOPS) as i:
        prev = ("down", 0)
        for j, (kind, c) in enumerate(FFN_BODY):
            run(i, n + j, kind, c, prev)
            prev = (kind, c)
    n += FFN_LOOPS * len(FFN_BODY)
    prev = ("down", 8)
    for kind, c in FFN_TAIL:
        run(None, n, kind, c, prev)
        prev = (kind, c)
        n += 1


def ffn_step_done(K, e, N, i, step):
    kind, c = step
    if kind == "up":
        e.wait_ge(N.up_mm, at(i, 4 * NPC, NPC * (c + 1)))
    else:
        e.wait_ge(N.down_mm, at(i, 2 * DN, DN * (c + 1)))


def ffn_pe(K, e, N, base, first=False):
    def run(i, n, kind, c, before):
        slot = (base + n) % 2
        e.wait_ge(K.w_lo, at(i, 12, 2 * (base + n + 1)))
        if kind == "up":
            whi = K.whi[:, slot].rearrange("p (m k n) -> p m k n", m=2, k=KT)
            wlo = K.wlo[:, slot].rearrange("p (m k n) -> p m k n", m=2, k=KT)
            for j, (a, b) in enumerate(PIECES):
                p = at(i, 4 * NPC, NPC * c + j)
                par = (NPC * c + j) % 2
                for m, done, free in ((0, N.gate_mm, N.silu), (1, N.up_mm, N.h32)):
                    wait(e, free, p - 1)
                    for k in range(KT):
                        if i is None and c == 0 and m == 0:
                            wait_normed(e, N, j, k)
                        mm = three(K, K.ps[:, 2 * m + par, :b - a], whi[:, m, k], wlo[:, m, k],
                                   K.nh[:, k, a:b], K.nl[:, k, a:b], k == 0, k == KT - 1)
                    mm.then_inc(done, 1)
                    if first and i is None and n == 0 and j == 0 and m == 0:
                        first_sum_pe(K, e, N, 2)
        else:
            whi = K.whi[:, slot].rearrange("p (r n) -> p r n", r=2)
            wlo = K.wlo[:, slot].rearrange("p (r n) -> p r n", r=2)
            e.wait_ge(N.hlo, at(i, 4 * NPC, 2 * NPC * (c + 1)))
            for d in range(KT):
                for j, (a, b) in enumerate(PIECES):
                    o = NPC * d + j
                    q = at(i, 2 * DN, DN * c + o)
                    wait(e, N.x_upd, q - 3)
                    for r in range(2):
                        mm = three(K, K.ps[:, 4 + o % 4, :b - a], whi[:, r, d * P:(d + 1) * P],
                                   wlo[:, r, d * P:(d + 1) * P], K.hh[:, c % 2, r, a:b],
                                   K.hl[:, c % 2, r, a:b], r == 0, r == 1)
                    mm.then_inc(N.down_mm, 1)
    ffn_steps(e, run)


def ffn_act(K, e, N, base, follow=None):
    nc = K.nc

    def hi(i, c, j):
        a, b = PIECES[j]
        p = NPC * c + j
        e.wait_ge(N.h32, at(i, 4 * NPC, p + 1))
        nc.scalar.copy(K.hh[:, (c // 2) % 2, c % 2, a:b], K.h32[:, p % 2, :b - a]).then_inc(N.hhi, 1)

    def run(i, n, kind, c, before):
        if before is None:
            K.before_split_act(e, N)
        else:
            ffn_step_done(K, e, N, i, before)
        if base + n + 1 < NSTEPS:
            split_hi(K, e, at(i, 6, base + n + 1), (base + n + 1) % 2)
        if kind == "up":
            for j, (a, b) in enumerate(PIECES):
                p = at(i, 4 * NPC, NPC * c + j)
                e.wait_ge(N.gate_mm, p + 1)
                wait(e, N.h32, p - 1)
                nc.scalar.activation(K.sg[:, (NPC * c + j) % 2, :b - a],
                                     K.ps[:, (NPC * c + j) % 2, :b - a], ACT.Silu).then_inc(N.silu, 1)
                if j:
                    hi(i, c, j - 1)
            hi(i, c, NPC - 1)
        elif follow and n == FFN_STEPS - 1:
            nc.scalar.preload_act_table_set(LOG_EXP)
            follow_act(K, e, follow, N.x_upd, DN * c)
    ffn_steps(e, run)


def ffn_dve(K, e, N, base):
    nc = K.nc

    def lo(i, c, j):
        a, b = PIECES[j]
        p = NPC * c + j
        e.wait_ge(N.hhi, at(i, 4 * NPC, p + 1))
        nc.vector.tensor_tensor(K.hl[:, (c // 2) % 2, c % 2, a:b], K.h32[:, p % 2, :b - a],
                                K.hh[:, (c // 2) % 2, c % 2, a:b].bitcast(F32),
                                ALU.subtract).then_inc(N.hlo, 1)

    def run(i, n, kind, c, before):
        def split(halves):
            if base + n + 1 < NSTEPS:
                split_lo(K, e, at(i, 6, base + n + 1), (base + n + 1) % 2, halves)

        if kind == "up":
            split((0, 1))
            for j, (a, b) in enumerate(PIECES):
                p = at(i, 4 * NPC, NPC * c + j)
                e.wait_ge(N.silu, p + 1)
                e.wait_ge(N.up_mm, p + 1)
                wait(e, N.hlo, p - 1)
                nc.vector.tensor_tensor(K.h32[:, (NPC * c + j) % 2, :b - a],
                                        K.sg[:, (NPC * c + j) % 2, :b - a],
                                        K.ps[:, 2 + (NPC * c + j) % 2, :b - a],
                                        ALU.mult).then_inc(N.h32, 1)
                if j:
                    lo(i, c, j - 1)
            lo(i, c, NPC - 1)
        else:
            for d in range(KT):
                for j, (a, b) in enumerate(PIECES):
                    o = NPC * d + j
                    q = at(i, 2 * DN, DN * c + o)
                    e.wait_ge(N.down_mm, q + 1)
                    nc.vector.scalar_tensor_tensor(out=K.x[:, d, a:b], in0=K.ps[:, 4 + o % 4, :b - a],
                                                   scalar=0.5, in1=K.x[:, d, a:b], op0=ALU.mult,
                                                   op1=ALU.add).then_inc(N.x_upd, 1)
                if d in (2, 4):
                    split((d // 4,))
    ffn_steps(e, run)


def proj_order(t):
    if t == 0:
        return [(m, j) for j in range(NPC) for m in range(len(IN_PLAN[t]))]
    return [(m, j) for m in range(len(IN_PLAN[t])) for j in range(NPC)]


def proj_pe(K, e, M, t):
    S = BASE_IN + t
    e.wait_ge(K.w_lo, 2 * (S + 1))
    plan = IN_PLAN[t]
    if isinstance(plan, str):
        whi = K.whi[:, S % 2].rearrange("p (k n) -> p k n", k=KT)
        wlo = K.wlo[:, S % 2].rearrange("p (k n) -> p k n", k=KT)
        for j, (a, r) in enumerate(TILES):
            n = IN_START[t] + j
            e.wait_ge(M.proj_read, max(n - 3, 1))
            for k in range(KT):
                mm = three(K, K.ps[:r, n % 4, :256], whi[:, k], wlo[:, k], K.nh[:, k, a:a + r],
                           K.nl[:, k, a:a + r], k == 0, k == KT - 1, token_major=True)
            mm.then_inc(M.proj_mm, 1)
            if plan == "fv":
                fox_sums_pe(K, e, M, j)
        return
    whi = K.whi[:, S % 2].rearrange("p (m k n) -> p m k n", m=2, k=KT)
    wlo = K.wlo[:, S % 2].rearrange("p (m k n) -> p m k n", m=2, k=KT)
    for n, (m, j) in enumerate(proj_order(t), IN_START[t]):
        a, b = PIECES[j]
        wait(e, M.proj_read, n - 3)
        for k in range(KT):
            if t == 0 and m == 0:
                wait_normed(e, M.norm, j, k)
            mm = three(K, K.ps[:, n % 4, :b - a], whi[:, m, k], wlo[:, m, k],
                       K.nh[:, k, a:b], K.nl[:, k, a:b], k == 0, k == KT - 1)
        mm.then_inc(M.proj_mm, 1)


def proj_act(K, e, M, t, parts):
    nc = K.nc
    if t == 0:
        K.before_split_proj(e, M)
    else:
        e.wait_ge(M.proj_mm, IN_START[t])
    split_hi(K, e, BASE_IN + t + 1, (BASE_IN + t + 1) % 2)
    plan = IN_PLAN[t]
    if -1 in parts:
        parts[-1]()
    if isinstance(plan, str):
        dst = K.fv if plan == "fv" else K.gv
        if plan == "gv":
            e.wait_ge(M.out, 16 * 3)
        for j, (a, r) in enumerate(TILES):
            n = IN_START[t] + j
            e.wait_ge(M.proj_mm, n + 1)
            nc.scalar.copy(dst[:r, j], K.ps[:r, n % 4, :256]).then_inc(M.proj_read, 1)
            if j in parts:
                parts[j]()
        return
    for n, (m, j) in enumerate(proj_order(t), IN_START[t]):
        name = plan[m]
        a, b = PIECES[j]
        e.wait_ge(M.proj_mm, n + 1)
        src = K.ps[:, n % 4, :b - a]
        if name == "z0" and j == 0:
            e.wait_ge(M.tail, 16)
            e.wait_ge(M.xc, 16)
        if name[0] == "x":
            u = int(name[1:])
            if j == 0:
                wait(e, M.conv, u - 1)
                wait(e, M.tail, 2 * (u - 1))
            if j < NPC - 1:
                nc.scalar.copy(K.raw[:, u % 2, 3 + a:3 + b], src).then_inc(M.proj_read, 1)
            else:
                nc.scalar.copy(K.raw[:, u % 2, 6 + TP:6 + b], src[:, TP - a:b - a])\
                    .then_inc(M.raw_tail, 1)
                nc.scalar.copy(K.raw[:, u % 2, 3 + a:3 + TP], src[:, :TP - a]).then_inc(M.proj_read, 1)
                conv_act(K, e, M, u - 1)
        elif name[0] == "z" or name[:2] == "gg":
            dst = (K.z if name[0] == "z" else K.gg)[:, int(name[-1]), a:b]
            nc.scalar.activation(dst, src, ACT.Silu).then_inc(M.proj_read, 1)
        else:
            if name == "gq" and j == 0:
                e.wait_ge(M.kout, 16)
            dst = {"fq0": K.fq[:, 0], "fq1": K.fq[:, 1], "fk0": K.fk[:, 0], "fk1": K.fk[:, 1],
                   "small": K.small, "gk": K.gk, "gq": K.gq}[name]
            nc.scalar.copy(dst[:, a:b], src).then_inc(M.proj_read, 1)
        if n - IN_START[t] in parts:
            parts[n - IN_START[t]]()
    if plan[-1] == "x7":
        conv_act(K, e, M, 7)


def conv_act(K, e, M, u):
    if u < 0:
        return
    e.wait_ge(M.conv, u + 1)
    b = K.vec[:, V_CB + u:V_CB + u + 1]
    K.nc.scalar.activation(K.xc[:, u, :TP], K.acc[:, u % 2, :TP], ACT.Silu, bias=b).then_inc(M.xc, 1)
    K.nc.scalar.activation(K.xc[:, u, TP:], K.acc[:, u % 2, TP + 3:TP + 3 + TS], ACT.Silu,
                           bias=b).then_inc(M.xc, 1)


def conv_dve(K, e, M, t):
    nc = K.nc
    L = T + 3
    for name in IN_PLAN[t]:
        u = int(name[1:])
        e.wait_ge(M.proj_read, IN_START[t] + NPC * (u % 2) + NPC)
        e.wait_ge(M.raw_tail, u + 1)
        e.wait_ge(M.prev, u + 1)
        wait(e, M.xc, 2 * (u - 1))
        acc = K.acc[:, u % 2]
        w = [K.vec[:, V_CW + 4 * u + q:V_CW + 4 * u + q + 1] for q in range(4)]
        M.dve(nc.vector.tensor_scalar(acc, K.raw[:, u % 2, 0:L], w[0], None, ALU.mult))
        for q in (1, 2):
            M.dve(nc.vector.scalar_tensor_tensor(out=acc, in0=K.raw[:, u % 2, q:q + L], scalar=w[q],
                                                 in1=acc, op0=ALU.mult, op1=ALU.add))
        nc.vector.scalar_tensor_tensor(out=acc, in0=K.raw[:, u % 2, 3:3 + L], scalar=w[3], in1=acc,
                                       op0=ALU.mult, op1=ALU.add).then_inc(M.conv, 1)


def conv_pool(K, e, M, out_tail):
    nc = K.nc
    for s in range(2):
        nc.gpsimd.memset(K.raw[:, s, 0:3], 0.0).then_inc(M.pad, 1)
    e.wait_ge(M.pad, 3)
    for u in range(8):
        wait(e, M.conv, u - 1)
        nc.gpsimd.tensor_copy(K.raw[:, u % 2, 3 + TP:6 + TP], K.cprev[:, u]).then_inc(M.prev, 1)
        e.wait_ge(M.raw_tail, u + 1)
        e.wait_ge(M.proj_read, IN_START[CONV_AT] + NPC * (u + 1))
        nc.gpsimd.tensor_copy(K.ctail[:, u, 0], K.raw[:, u % 2, TP:TP + 3]).then_inc(M.tail, 1)
        nc.gpsimd.tensor_copy(K.ctail[:, u, 1], K.raw[:, u % 2, 3 + T:6 + T]).then_inc(M.tail, 1)
    e.wait_ge(M.tail, 16)
    e.dma_start(out_tail, K.ctail[:]).then_inc(M.out, 16)


def softplus_exp_act(K, e, s, a):
    e.wait_ge(s.absv, 1)
    K.nc.scalar.activation(a, a, ACT.Exp, scale=-1.0).then_inc(s.e, 1)


def softplus_ln_act(K, e, s, b):
    e.wait_ge(s.u, 1)
    K.nc.scalar.activation(b, b, ACT.Ln).then_inc(s.ln, 1)


def softplus_dve(K, e, M, s, v, a, b):
    V = K.nc.vector
    V.scalar_tensor_tensor(out=a, in0=v, scalar=-1.0, in1=v, op0=ALU.mult, op1=ALU.max).then_inc(s.absv, 1)
    e.wait_ge(s.e, 1)
    M.dve(V.tensor_scalar(b, a, 1.0, None, ALU.add))
    V.scalar_tensor_tensor(out=a, in0=b, scalar=-1.0, in1=a, op0=ALU.add, op1=ALU.subtract).then_inc(s.u, 1)
    e.wait_ge(s.ln, 1)
    M.dve(V.tensor_tensor(a, b, a, ALU.subtract))


FOX_UNITS = [(h, j) for h in range(FOX_H) for j in range(NTT)]
PR = 4
NU = len(FOX_UNITS)
BIAS_AT = 4


def bias_bank(it, q):
    return 2 * ((it + 1) % 2) + q % 2 if it >= 0 else 6 + q % 2


def fox_keys(j):
    return PAST + TS if j == NTT - 1 else P * (j + 1)


def fox_groups(j):
    n = fox_keys(j)
    tiles = [(k, min(P, n - k)) for k in range(0, n, P)]
    return [tiles[g:g + 4] for g in range(0, len(tiles), 4)]


FOX_G = [0]
for _h, _j in FOX_UNITS:
    FOX_G.append(FOX_G[-1] + len(fox_groups(_j)))
FOX_QK = [(n // NPC, PIECES[n % NPC]) for n in range(4 * NPC)]


def fox_tile(K, m):
    return K.fq[:, m] if m < 2 else K.fk[:, m - 2]


FOX_NORM = ((0,), (1, 2), (3,), (4, 5), (6,), (7,), (8, 9), (10,), (11,))


def fox_sums_pe(K, e, M, j):
    for n in FOX_NORM[j]:
        m, (a, b) = FOX_QK[n]
        e.wait_ge(M.fsq, n + 1)
        wait(e, M.fln, n - 1)
        K.nc.tensor.matmul(K.ps[:, 4 + n % 2, :b - a], K.b64, K.sq[:, n % 2, :b - a],
                           start=True, stop=True).then_inc(M.fss, 1)


def fox_pe(K, e, M):
    nc = K.nc
    def bias(h, it):
        wait(e, M.smin, it)
        for q in range(4):
            n = 4 * h + q
            if n == 0:
                e.wait_ge(M.cum, 1)
            wait(e, M.cb, n - 1)
            nc.tensor.matmul(K.ps[:, bias_bank(it, q), :400], K.const[:, C_SEL + h * P:C_SEL + (h + 1) * P],
                             K.cum[:, 400 * q:400 * q + 400],
                             start=True, stop=True).then_inc(M.cb_mm, 1)

    def scores(u):
        h, j = FOX_UNITS[u]
        a, r = TILES[j]
        q = K.qz[:, u % 2, :r]
        e.wait_ge(M.qz, u + 1)
        wait(e, M.smin, u - 1)
        if u == 0 or FOX_UNITS[u - 1][1] == BIAS_AT and h < FOX_H - 1:
            e.wait_ge(M.cb, 4 * (h + 1 + (u > 0)))
        if j < NTT - 1:
            n = fox_keys(j)
            parts = [(k, min(512, n - k), K.fk[:, h // 2, k:min(k + 512, n)]) for k in range(0, n, 512)]
        else:
            parts = [(0, PAST, K.kc[:, h // 2, :]), (PAST, TS, K.fk[:, h // 2, TP:T])]
        for k, n, rhs in parts:
            mm = nc.tensor.matmul(K.psf[:r, 1024 * (u % 2) + k:1024 * (u % 2) + k + n], q, rhs,
                                  start=True, stop=True)
        mm.then_inc(M.s_mm, 1)

    def turn(u):
        h, j = FOX_UNITS[u]
        r = TILES[j][1]
        e.wait_ge(M.p_scaled, u + 1)
        for g, tiles in enumerate(fox_groups(j)):
            n = FOX_G[u] + g
            wait_pt(n - 2)
            for i, (k, w) in enumerate(tiles):
                mm = nc.tensor.transpose(K.ps[:w, 4 + n % 2, i * P:i * P + r], K.pr[u % PR][:r, k:k + w],
                                         K.ident[:r, :r])
            mm.then_inc(M.pt_mm, 1)

    def wait_pt(n):
        if n < 0:
            return
        u = max(v for v in range(NU) if FOX_G[v] <= n)
        if n == FOX_G[u]:
            e.wait_ge(M.pt_a, u + 1)
        else:
            e.wait_ge(M.pt_v, K.second(u) + 1)

    def values(u):
        h, j = FOX_UNITS[u]
        r = TILES[j][1]
        o = 64 * (h % 2)
        e.wait_ge(M.pt_a, u + 1)
        wait(e, M.pt_v, K.second(u + 1))
        wait(e, M.fo, u - 1)
        tiles = [x for g in fox_groups(j) for x in g]
        for i, (k, w) in enumerate(tiles):
            if j == NTT - 1:
                v = K.vc[:, i, 64 * h:64 * h + 64] if i < PAST // P else K.fv[:TS, j, 64 * h:64 * h + 64]
            else:
                v = K.fv[:, i, 64 * h:64 * h + 64]
            mm = nc.tensor.matmul(K.ps[o:o + 64, 6 + u % 2, :r], v, K.pt[:w, u % 2, i, :r],
                                  start=i == 0, stop=i == len(tiles) - 1)
        mm.then_inc(M.o_mm, 1)

    bias(0, -1)
    e.wait_ge(M.fqk, len(FOX_QK))
    e.wait_ge(M.cache, 16 * 3)
    e.wait_ge(M.proj_read, IN_START[FOX_AT])
    for it in range(NU + PR):
        if it < NU:
            scores(it)
            h, j = FOX_UNITS[it]
            if j == BIAS_AT and h + 1 < FOX_H:
                bias(h + 1, it)
        if 0 <= it - (PR - 1) < NU:
            turn(it - (PR - 1))
        if 0 <= it - PR < NU:
            values(it - PR)


def fox_small_act(K, e, M):
    return {NPC: lambda: softplus_exp_act(K, e, M.sp, K.t1), NPC + 1: lambda: softplus_ln_act(K, e, M.sp, K.t2)}


def fox_norm_act(K, e, M):
    def square(n):
        m, (a, b) = FOX_QK[n]
        wait(e, M.fss, n - 1)
        K.nc.scalar.activation(K.sq[:, n % 2, :b - a], fox_tile(K, m)[:, a:b], ACT.Square).then_inc(M.fsq, 1)

    def first():
        square(0)
        square(1)

    def after(j):
        for n in FOX_NORM[j]:
            rstd(K, e, M, n)
            if n + 2 < len(FOX_QK):
                square(n + 2)

    parts = {j: lambda j=j: after(j) for j in range(NTT)}
    parts[-1] = first
    return parts


def fox_act(K, e, M):
    nc = K.nc

    def bias(h, it):
        for q in range(4):
            n = 4 * h + q
            e.wait_ge(M.cb_mm, n + 1)
            nc.scalar.copy(K.cb[:, h % 2, 400 * q:400 * q + 400], K.ps[:, bias_bank(it, q), :400]).then_inc(M.cb, 1)

    def turned(u):
        h, j = FOX_UNITS[u]
        r = TILES[j][1]
        e.wait_ge(M.pt_mm, FOX_G[u] + 1)
        wait(e, M.o_mm, u - 1)
        n = len(fox_groups(j)[0])
        nc.scalar.copy(K.pt[:, u % 2, :n, :r],
                       K.ps[:, 4 + FOX_G[u] % 2].rearrange("p (n q) -> p n q", q=P)[:, :n, :r])\
            .then_inc(M.pt_a, 1)

    bias(0, -1)
    for it in range(NU + PR - 1):
        if it < NU:
            h, j = FOX_UNITS[it]
            if j == BIAS_AT and h + 1 < FOX_H:
                bias(h + 1, it)
        if it >= PR - 1:
            turned(it - (PR - 1))
        if it < NU:
            r = TILES[j][1]
            n = fox_keys(j)
            e.wait_ge(M.smin, it + 1)
            nc.scalar.activation(K.pr[it % PR][:r, :n], K.pr[it % PR][:r, :n], ACT.Exp, bias=K.mn[:r, it % PR:it % PR + 1],
                                 scale=-1.0, accum_out=K.rs[:r, it % PR:it % PR + 1]).then_inc(M.p_exp, 1)


def rstd(K, e, M, n):
    a, b = FOX_QK[n][1]
    e.wait_ge(M.fss, n + 1)
    wait(e, M.frs, n)
    K.nc.scalar.activation(K.lnv[:, :b - a], K.ps[:, 4 + n % 2, :b - a], ACT.Ln, bias=K.eps[:, 0:1],
                           scale=1.0 / FOX_D).then_inc(M.fln, 1)
    e.wait_ge(M.fln, n + 1)
    wait(e, M.fqk, n - 1)
    K.nc.scalar.activation(K.n32[:, n % 2, :b - a], K.lnv[:, :b - a], ACT.Exp, scale=-0.5).then_inc(M.frs, 1)


def fox_small_dve(K, e, M):
    V = K.nc.vector
    e.wait_ge(M.proj_read, IN_START[2] + NPC)
    e.wait_ge(M.x_out, 16)
    M.dve(V.tensor_scalar(K.small[:], K.small[:], K.vec[:, V_SB:V_SB + 1], None, ALU.add))
    softplus_dve(K, e, M, M.sp, K.small[:], K.t1, K.t2)
    f = slice(SMALL_FF, SMALL_FF + FOX_H)
    g = slice(SMALL_DT, SMALL_DT + SSD_H)
    V.scalar_tensor_tensor(out=K.small[f, :], in0=K.small[f, :], scalar=0.0, in1=K.t1[f, :],
                           op0=ALU.min, op1=ALU.subtract).then_inc(M.logf, 1)
    M.dve(V.scalar_tensor_tensor(out=K.small[g, :], in0=K.small[g, :], scalar=0.0, in1=K.t1[g, :],
                                 op0=ALU.max, op1=ALU.add))
    e.wait_ge(M.logf, 1)
    e.wait_ge(M.cache, 16 * 3)
    ones = K.t2[f, :TP]
    M.dve(V.memset(ones, 1.0))
    M.dve(V.memset(K.cum[:], 0.0))
    M.dve(V.tensor_tensor_scan(K.cum[f, 0:TP], ones, K.small[f, 0:TP], 0.0, ALU.mult, ALU.add))
    M.dve(V.tensor_tensor_scan(K.cum[f, TP:TP + PAST], ones[:, :PAST], K.lfc[f, :], 0.0, ALU.mult, ALU.add))
    V.tensor_tensor_scan(K.cum[f, TP + PAST:], ones[:, :TS], K.small[f, TP:T],
                         K.cum[f, TP + PAST - 1:TP + PAST], ALU.mult, ALU.add).then_inc(M.cum, 1)


def fox_norm_dve(K, e, M):
    V = K.nc.vector
    for n, (m, (a, b)) in enumerate(FOX_QK):
        gain = V_QN if m < 2 else V_KN
        e.wait_ge(M.frs, n + 1)
        V.scalar_tensor_tensor(out=fox_tile(K, m)[:, a:b], in0=fox_tile(K, m)[:, a:b],
                               scalar=K.vec[:, gain:gain + 1], in1=K.n32[:, n % 2, :b - a],
                               op0=ALU.mult, op1=ALU.mult).then_inc(M.fqk, 1)


def fox_dve(K, e, M):
    nc = K.nc
    V = nc.vector
    for it in range(NU + PR):
        if it < NU:
            h, j = FOX_UNITS[it]
            r = TILES[j][1]
            n = fox_keys(j)
            e.wait_ge(M.s_mm, it + 1)
            e.wait_ge(M.cb, 4 * (h + 1))
            if it >= PR:
                e.wait_ge(M.pt_mm, FOX_G[it - PR + 1])
            s = K.psf[:r, 1024 * (it % 2):1024 * (it % 2) + n]
            M.dve(V.tensor_tensor(s[:, n - r:n], s[:, n - r:n], K.mqk[:r, :r], ALU.add))
            c0 = 0 if j < NTT - 1 else TP
            V.tensor_tensor_reduce(out=K.pr[it % PR][:r, :n], in0=s, in1=K.cb[:r, h % 2, c0:c0 + n],
                                   scale=-0.125, scalar=3e38, op0=ALU.add, op1=ALU.min,
                                   accum_out=K.mn[:r, it % PR:it % PR + 1]).then_inc(M.smin, 1)
        if 1 <= it <= NU:
            u = it - 1
            r = TILES[FOX_UNITS[u][1]][1]
            e.wait_ge(M.p_exp, u + 1)
            wait(e, M.p_scaled, u - PR + 1)
            V.reciprocal(K.ri[:r, u % PR:u % PR + 1], K.rs[:r, u % PR:u % PR + 1]).then_inc(M.rinv, 1)
        if 0 <= it - (PR - 1) < NU:
            u = it - (PR - 1)
            h, j = FOX_UNITS[u]
            r = TILES[j][1]
            gs = fox_groups(j)
            if len(gs) > 1:
                n = FOX_G[u] + 1
                e.wait_ge(M.pt_mm, n + 1)
                wait(e, M.o_mm, u - 1)
                m, w = len(gs[1]), gs[1][0][1]
                V.tensor_copy(K.pt[:w, u % 2, 4:4 + m, :r],
                              K.ps[:w, 4 + n % 2].rearrange("p (n q) -> p n q", q=P)[:, :m, :r])\
                    .then_inc(M.pt_v, 1)
        if 0 <= it - PR < NU:
            u = it - PR
            h, j = FOX_UNITS[u]
            a, r = TILES[j]
            o = 64 * (h % 2)
            e.wait_ge(M.o_mm, u + 1)
            if u == 0:
                e.wait_ge(M.kout, 16)
            V.tensor_copy(K.fq[o:o + 64, h // 2, a:a + r], K.ps[o:o + 64, 6 + u % 2, :r])\
                .then_inc(M.fo, 1)


def fox_pool(K, e, M, outs):
    nc = K.nc
    e.wait_ge(M.proj_read, IN_START[FOX_AT])
    for j in range(2):
        src = K.fv[:, :TP // P] if j == 0 else K.fv[:TS, TP // P:TP // P + 1]
        e.dma_start(outs["v"][j], src).then_inc(M.out, 16)
    e.wait_ge(M.logf, 1)
    e.dma_start(outs["logf"], K.small[SMALL_FF:SMALL_FF + FOX_H, :]).then_inc(M.out, 16)
    e.wait_ge(M.fqk, len(FOX_QK))
    e.dma_start(outs["k"], K.fk[:]).then_inc(M.kout, 16)

    def one_head(u):
        h, j = FOX_UNITS[u]
        a, r = TILES[j]
        wait(e, M.s_mm, u - 1)
        nc.gpsimd.tensor_scalar(K.qz[:, u % 2, :r], K.fq[:, h // 2, a:a + r],
                                K.b64[:, 64 * (h % 2):64 * (h % 2) + 1], 1.0, ALU.mult, ALU.mult).then_inc(M.qz, 1)

    for u in range(2):
        one_head(u)
    for u, (h, j) in enumerate(FOX_UNITS):
        r = TILES[j][1]
        n = fox_keys(j)
        if u + 2 < NU:
            one_head(u + 2)
        e.wait_ge(M.rinv, u + 1)
        nc.gpsimd.tensor_scalar(K.pr[u % PR][:r, :n], K.pr[u % PR][:r, :n], K.ri[:r, u % PR:u % PR + 1], 1.0,
                                ALU.mult, ALU.mult).then_inc(M.p_scaled, 1)


GLA_L = 64
GCH = T // GLA_L


def gla_gate_pe(K, e, M):
    e.wait_ge(M.fo, NU)
    for j, (a, b) in enumerate(PIECES):
        K.nc.tensor.matmul(K.ps[:, 4 + j, :b - a], K.const[:GLA_R, C_SEL:C_SEL + P], K.small[:GLA_R, a:b],
                           start=True, stop=True).then_inc(M.g_mm, 1)


def gla_pe(K, e, M):
    nc = K.nc
    e.wait_ge(M.proj_read, IN_START[GLA_AT])
    e.wait_ge(M.kend, 1)
    for g in range(0, NTT, 4):
        for j in range(g, min(g + 4, NTT)):
            a, r = TILES[j]
            mm = nc.tensor.transpose(K.ps[:r, 4 + g // 4, P * (j - g):P * (j - g) + P], K.ge[:, a:a + r], K.ident)
        mm.then_inc(M.kt_mm, 1)
    e.wait_ge(M.gqk, 1)

    def scores(j):
        a, r = TILES[j]
        wait(e, M.att, j - 1)
        e.wait_ge(M.gqm, j + 1)
        nc.tensor.matmul(K.ps[:r, j % 2].rearrange("p (h q) -> p h q", h=GLA_H)[:, :, :r], K.gk[:, a:a + r],
                         K.gqm[:, j % 2, :, :r], start=True, stop=True).then_inc(M.att_mm, 1)

    def states(j):
        for s in range(TILES[j][1] // GLA_L):
            c = 2 * j + s
            o = GLA_L * s
            wait(e, M.st_read, c - 1)
            nc.tensor.matmul(K.ps[:, 6 + s, :256], K.kt[o:o + GLA_L, j], K.gv[o:o + GLA_L, j],
                             start=True, stop=True).then_inc(M.st_mm, 1)

    def outputs(j):
        a, r = TILES[j]
        wait(e, M.go_read, j - 1)
        out = K.ps[:, 4 + j % 2, :256].rearrange("p (t q) -> p t q", t=2)
        first = True
        for s in range(r // GLA_L):
            c = 2 * j + s
            e.wait_ge(M.S, c + 1)
            for t in range(2):
                nc.tensor.matmul(out[:, t, GLA_L * s:GLA_L * s + GLA_L], K.S[:, c % 4, P * t:P * t + P],
                                 K.gq[:, a + GLA_L * s:a + GLA_L * s + GLA_L], start=first, stop=False,
                                 skip_group_check=True)
                first = False
        e.wait_ge(M.att, j + 1)
        for h in range(GLA_H):
            o = 64 * (h % 2)
            mm = nc.tensor.matmul(out[o:o + 64, h // 2, :r], K.gv[:r, j, 64 * h:64 * h + 64], K.attn[:r, j % 2, h, :r],
                                  start=False, stop=h == GLA_H - 1, skip_group_check=True)
        mm.then_inc(M.go_mm, 1)

    scores(0)
    e.wait_ge(M.kt_read, 3)
    states(0)
    for j in range(NTT):
        if j + 1 < NTT:
            scores(j + 1)
            states(j + 1)
        outputs(j)
    e.wait_ge(M.go_read, NTT)
    for n in range(2 * NPC):
        a, b = PIECES[n % NPC]
        e.wait_ge(M.gsq, n + 1)
        wait(e, M.gln, n - 1)
        nc.tensor.matmul(K.ps[:, 4 + n % 2, :b - a], K.b64, K.sq[:, n % 2, :b - a],
                         start=True, stop=True).then_inc(M.gss, 1)


def gla_gate_act(K, e, M):
    nc = K.nc
    g = slice(SMALL_DT, SMALL_DT + SSD_H)

    def exp_b():
        e.wait_ge(M.bcum, 1)
        nc.scalar.activation(K.ga[:], K.ge[:], ACT.Exp).then_inc(M.eb, 1)
        nc.scalar.activation(K.gb[:], K.ge[:], ACT.Exp, scale=-1.0).then_inc(M.enb, 1)

    def exp_last():
        e.wait_ge(M.bdiff, 1)
        nc.scalar.activation(K.gd[:], K.gd[:], ACT.Exp).then_inc(M.ebd, 1)
        nc.scalar.activation(K.eal[g, 0:1], K.vec[g, V_AL:V_AL + 1], ACT.Exp).then_inc(M.ealog, 1)

    return {0: lambda: softplus_exp_act(K, e, M.gsp, K.ga[:]), 2: lambda: softplus_ln_act(K, e, M.gsp, K.gb[:]),
            5: exp_b, 6: exp_last}


def gla_act(K, e, M):
    nc = K.nc
    for g in range(0, NTT, 4):
        e.wait_ge(M.kt_mm, g // 4 + 1)
        n, r = (4, P) if g + 4 < NTT else (1, TS)
        nc.scalar.copy(K.kt[:r, g:g + n], K.ps[:r, 4 + g // 4, :P * n].rearrange("p (n q) -> p n q", q=P))\
            .then_inc(M.kt_read, 1)
    nc.scalar.preload_act_table_set(LOG_EXP)
    for j, (a, r) in enumerate(TILES):
        e.wait_ge(M.go_mm, j + 1)
        nc.scalar.copy(K.go[:, :, a:a + r], K.ps[:, 4 + j % 2, :256].rearrange("p (t q) -> p t q", t=2)[:, :, :r])\
            .then_inc(M.go_read, 1)
    e.wait_ge(M.go_read, NTT)
    for n in range(2 * NPC + 1):
        if n < 2 * NPC:
            a, b = PIECES[n % NPC]
            wait(e, M.gss, n - 1)
            nc.scalar.activation(K.sq[:, n % 2, :b - a], K.go[:, n // NPC, a:b], ACT.Square).then_inc(M.gsq, 1)
        if n:
            m = n - 1
            a, b = PIECES[m % NPC]
            e.wait_ge(M.gss, m + 1)
            wait(e, M.grs, m)
            nc.scalar.activation(K.lnv[:, :b - a], K.ps[:, 4 + m % 2, :b - a], ACT.Ln, bias=K.eps[:, 0:1],
                                 scale=1.0 / GLA_V).then_inc(M.gln, 1)
            e.wait_ge(M.gln, m + 1)
            wait(e, M.gnorm, m - 1)
            nc.scalar.activation(K.n32[:, m % 2, :b - a], K.lnv[:, :b - a], ACT.Exp, scale=-0.5).then_inc(M.grs, 1)


def gla_gate_dve(K, e, M):
    nc = K.nc
    V = nc.vector
    ch = lambda t: t[:].rearrange("p (c l) -> p c l", l=GLA_L)
    e.wait_ge(M.g_mm, NPC)
    for j, (a, b) in enumerate(PIECES):
        M.dve(V.tensor_scalar(K.gd[:, a:b], K.ps[:, 4 + j, :b - a], K.vec[:, V_GB:V_GB + 1], None, ALU.add))
    softplus_dve(K, e, M, M.gsp, K.gd[:], K.ga[:], K.gb[:])
    M.dve(V.scalar_tensor_tensor(out=K.gd[:], in0=K.gd[:], scalar=0.0, in1=K.ga[:], op0=ALU.min, op1=ALU.subtract))
    M.dve(V.tensor_scalar(K.gd[:], K.gd[:], 1.0 / GLA_TAU, None, ALU.mult))
    M.dve(V.memset(K.ga[:], 1.0))
    M.dve(V.memset(ch(K.ga)[:, :, 0:1], 0.0))
    V.tensor_tensor_scan(K.ge[:], K.ga[:], K.gd[:], 0.0, ALU.mult, ALU.add).then_inc(M.bcum, 1)
    e.wait_ge(M.bcum, 1)
    V.tensor_tensor(ch(K.gd), ch(K.ge)[:, :, GLA_L - 1:GLA_L].to_broadcast([P, GCH, GLA_L]), ch(K.ge),
                    ALU.subtract).then_inc(M.bdiff, 1)
    e.wait_ge(M.eb, 1)
    e.wait_ge(M.proj_read, IN_START[GLA_GATE_AT])
    M.dve(V.tensor_copy(K.glast[:], ch(K.ga)[:, :, GLA_L - 1]))
    M.dve(V.scalar_tensor_tensor(out=K.gq[:], in0=K.gq[:], scalar=float(GLA_K) ** -0.5, in1=K.ga[:],
                                 op0=ALU.mult, op1=ALU.mult))
    e.wait_ge(M.ebd, 1)
    e.wait_ge(M.enb, 1)
    V.tensor_tensor(K.ge[:], K.gk[:], K.gd[:], ALU.mult).then_inc(M.kend, 1)
    e.wait_ge(M.kend, 1)
    V.tensor_tensor(K.gk[:], K.gk[:], K.gb[:], ALU.mult).then_inc(M.gqk, 1)


def gla_dve(K, e, M):
    nc = K.nc
    V = nc.vector
    M.dve(V.memset(K.attn[:], 0.0))
    V.memset(K.S[:, 0], 0.0).then_inc(M.S, 1)
    e.wait_ge(M.S, 1)

    def masked(j):
        a, r = TILES[j]
        e.wait_ge(M.att_mm, j + 1)
        wait(e, M.go_mm, j - 1)
        V.copy_predicated(K.attn[:r, j % 2, :, :r], K.gmask[:r, :r].rearrange("p (o q) -> p o q", o=1)
                          .to_broadcast([r, GLA_H, r]),
                          K.ps[:r, j % 2].rearrange("p (h q) -> p h q", h=GLA_H)[:, :, :r]).then_inc(M.att, 1)

    masked(0)
    for j, (a, r) in enumerate(TILES):
        for s in range(r // GLA_L):
            c = 2 * j + s
            e.wait_ge(M.st_mm, c + 1)
            V.tensor_tensor(K.gst, K.ps[:, 6 + s, :256], K.bmask, ALU.mult).then_inc(M.st_read, 1)
            e.wait_ge(M.st_read, c + 1)
            if c == TP // GLA_L - 1:
                M.dve(V.scalar_tensor_tensor(out=K.Sp[:], in0=K.S[:, c % 4], scalar=K.glast[:, c:c + 1],
                                             in1=K.gst, op0=ALU.mult, op1=ALU.add))
                e.wait_ge(M.go_mm, (c - 3) // 2 + 1)
                e.wait_ge(M.cache, 16 * (3 + GLA_H))
                V.tensor_copy(K.S[:, (c + 1) % 4], K.Sin).then_inc(M.S, 1)
                e.wait_ge(M.S, c + 2)
            elif c == GCH - 1:
                V.scalar_tensor_tensor(out=K.Ss, in0=K.S[:, c % 4], scalar=K.glast[:, c:c + 1],
                                       in1=K.gst, op0=ALU.mult, op1=ALU.add).then_inc(M.S_end, 1)
            else:
                if c >= 3:
                    e.wait_ge(M.go_mm, (c - 3) // 2 + 1)
                V.scalar_tensor_tensor(out=K.S[:, (c + 1) % 4], in0=K.S[:, c % 4], scalar=K.glast[:, c:c + 1],
                                       in1=K.gst, op0=ALU.mult, op1=ALU.add).then_inc(M.S, 1)
                e.wait_ge(M.S, c + 2)
        if j + 1 < NTT:
            masked(j + 1)
    for n in range(2 * NPC):
        a, b = PIECES[n % NPC]
        e.wait_ge(M.grs, n + 1)
        o = K.go[:, n // NPC, a:b]
        V.scalar_tensor_tensor(out=o, in0=o, scalar=K.vec[:, V_GN:V_GN + 1], in1=K.n32[:, n % 2, :b - a],
                               op0=ALU.mult, op1=ALU.mult).then_inc(M.gnorm, 1)
        e.wait_ge(M.gnorm, n + 1)
        V.tensor_tensor(K.gg[:, n // NPC, a:b], o, K.gg[:, n // NPC, a:b], ALU.mult).then_inc(M.gout, 1)


def gla_pool(K, e, M, outs):
    heads = K.bmask.rearrange("p (h v) -> p h v", h=GLA_H)[:, :, 0:1]
    for j, (a, r) in enumerate(TILES):
        wait(e, M.att_mm, j - 1)
        K.nc.gpsimd.tensor_tensor(K.gqm[:, j % 2, :, :r],
                                  K.gq[:, a:a + r].rearrange("p (o q) -> p o q", o=1).to_broadcast([P, GLA_H, r]),
                                  heads.to_broadcast([P, GLA_H, r]), ALU.mult).then_inc(M.gqm, 1)
    e.wait_ge(M.S_end, 1)
    for j, src in enumerate((K.Sp, K.Ss)):
        for h in range(GLA_H):
            o = GLA_K * h
            e.dma_start(outs["gla"][j, o:o + GLA_K], src[o:o + GLA_K, 64 * h:64 * h + 64]).then_inc(M.out, 16)


Y_PIECES = [(a, min(a + 2 * P, T)) for a in range(0, T, 2 * P)]
NYP = len(Y_PIECES)


def y_after(j, lag):
    c, odd = divmod(j - lag - 1, 2)
    return c if not odd and 0 <= c < NYP - 2 else None


def ssd_pe(K, e, M):
    nc = K.nc
    g = slice(SMALL_DT, SMALL_DT + SSD_H)
    e.wait_ge(M.proj_read, IN_START[IN_STEPS])
    e.wait_ge(M.acum, 1)
    e.wait_ge(M.xc, 16)
    e.wait_ge(M.H, 1)

    def front(j):
        a, r = TILES[j]
        wait(e, M.seg, j)
        wait(e, M.ea, j)
        wait(e, M.de0, j)
        for h in range(SSD_H):
            mm = nc.tensor.matmul(K.psf[:, P * h:P * h + r], K.const[:, C_SEL + P * h:C_SEL + P * h + P],
                                  K.adt[:, a:a + r], start=True, stop=True)
        mm.then_inc(M.a_mm, 1)
        wait(e, M.b_read, j)
        wait(e, M.sm_read, j)
        for u in range(2):
            nc.tensor.transpose(K.ps[:r, 3, P * u:P * u + P], K.xc[:, 4 + u, a:a + r], K.ident)
        nc.tensor.transpose(K.ps[:r, 3, 256:264], K.adt[g, a:a + r], K.ident[g, g])
        nc.tensor.transpose(K.ps[:r, 3, 264:272], K.small[g, a:a + r], K.ident[g, g]).then_inc(M.b_mm, 1)
        wait(e, M.x_read, j)
        for u in range(4):
            mm = nc.tensor.transpose(K.ps[:r, 2, P * u:P * u + P], K.xc[:, u, a:a + r], K.ident)
        mm.then_inc(M.x_mm, 1)

    def cb(j):
        a, r = TILES[j]
        wait(e, M.m, j)
        for u in range(2):
            mm = nc.tensor.matmul(K.ps[:r, 4, P * u:P * u + r], K.xc[:, 4 + u, a:a + r],
                                  K.xc[:, 6 + u, a:a + r], start=True, stop=True)
        mm.then_inc(M.cb2_mm, 1)

    def sums(c):
        a, b = Y_PIECES[c]
        e.wait_ge(M.ysq, c + 1)
        wait(e, M.yln, c)
        for g in range(2):
            for u in range(2):
                mm = nc.tensor.matmul(K.ps[:, 7, 256 * g:256 * g + b - a], K.ones, K.ysq[:, 2 * g + u, :b - a],
                                      start=u == 0, stop=u == 1)
        mm.then_inc(M.yss, 1)

    def back(j):
        a, r = TILES[j]
        wait(e, M.y1, j)
        e.wait_ge(M.cea, j + 1)
        wait(e, M.hst_read, j)
        if j == NTT - 1:
            e.wait_ge(M.H, 2)
        y = K.ps[:, 5].rearrange("p (t q) -> p t q", t=4)
        for h in range(SSD_H):
            o = 64 * (h % 2)
            mm = nc.tensor.matmul(y[o:o + 64, h // 2, :r], K.H[:, 64 * h:64 * h + 64], K.cea[:, j % 2, h, :r],
                             start=h < 2, stop=False, skip_group_check=True)
        mm.then_inc(M.h_read, 1)
        e.wait_ge(M.b_read, j + 1)
        e.wait_ge(M.x_read, j + 1)
        for u in range(2):
            mm = nc.tensor.matmul(K.ps[:, 6, 256 * u:256 * u + 256], K.btok[:r, P * u:P * u + P],
                                  K.xde[:r, 256 * u:256 * u + 256], start=True, stop=True)
        mm.then_inc(M.hst_mm, 1)
        e.wait_ge(M.m, j + 1)
        e.wait_ge(M.xdt, j + 1)
        for h in range(SSD_H):
            o = 64 * (h % 2)
            mm = nc.tensor.matmul(y[o:o + 64, h // 2, :r], K.xdt[:r, 64 * h:64 * h + 64], K.seg[:r, j % 2, h, :r],
                                  start=False, stop=h >= 6, skip_group_check=True)
        mm.then_inc(M.y_mm, 1)

    front(0)
    cb(0)
    for j in range(NTT):
        if j + 1 < NTT:
            front(j + 1)
        back(j)
        if j + 1 < NTT:
            cb(j + 1)
        if y_after(j, 2) is not None:
            sums(y_after(j, 2))
    sums(NYP - 2)
    sums(NYP - 1)


def ssd_act(K, e, M):
    nc = K.nc
    nc.scalar.preload_act_table_set(LOG_EXP)

    def square(c):
        a, b = Y_PIECES[c]
        e.wait_ge(M.y2, min(2 * c + 2, NTT))
        wait(e, M.yss, c)
        nc.scalar.activation(K.ysq[:, :, :b - a], K.z[:, :, a:b], ACT.Square).then_inc(M.ysq, 1)

    def rms(c):
        w = Y_PIECES[c][1] - Y_PIECES[c][0]
        e.wait_ge(M.yss, c + 1)
        wait(e, M.ynorm, c)
        nc.scalar.activation(K.yrms[:, :, :w], K.ps[:, 7].rearrange("p (g q) -> p g q", g=2)[:, :, :w], ACT.Ln,
                             bias=K.eps[:, 0:1], scale=1.0 / 256).then_inc(M.yln, 1)
        e.wait_ge(M.yln, c + 1)
        nc.scalar.activation(K.yrms[:, :, :w], K.yrms[:, :, :w], ACT.Exp, scale=-0.5).then_inc(M.yrs, 1)

    for j, (a, r) in enumerate(TILES):
        e.wait_ge(M.de0, j + 1)
        nc.scalar.activation(K.de[:r, 0:8], K.de[:r, 0:8], ACT.Exp).then_inc(M.de1, 1)
        e.wait_ge(M.seg, j + 1)
        wait(e, M.cea, j - 1)
        wait(e, M.hupd, j - 1)
        nc.scalar.activation(K.ea[:, j % 2, :, :r],
                             K.psf[:, :1024].rearrange("p (h q) -> p h q", h=SSD_H)[:, :, :r],
                             ACT.Exp).then_inc(M.ea, 1)
        nc.scalar.activation(K.seg[:r, j % 2, :, :r], K.seg[:r, j % 2, :, :r], ACT.Exp).then_inc(M.eseg, 1)
        wait(e, M.hst_mm, j)
        nc.scalar.copy(K.btok[:r, :], K.ps[:r, 3, 0:256]).then_inc(M.b_read, 1)
        if y_after(j, 2) is not None:
            square(y_after(j, 2))
        if y_after(j, 3) is not None:
            rms(y_after(j, 3))
        if j >= 2 and j - 2 < len(MIX_EARLY):
            k = MIX_EARLY[j - 2]
            if k < 6:
                e.wait_ge(M.gout, 2 * NPC)
            nc.scalar.copy(K.nh[:, k], mixed_tile(K, k)).then_inc(M.mhi_early, 1)
    square(NYP - 2)
    e.wait_ge(M.h_read, NTT)
    e.wait_ge(M.y_mm, NTT)
    e.wait_ge(M.hupd, NTT)
    e.wait_ge(M.hst_mm, NTT)
    ssd_hi(K, e, M, 0)
    rms(NYP - 2)
    square(NYP - 1)
    ssd_hi(K, e, M, 1)
    rms(NYP - 1)
    ssd_hi(K, e, M, 2)


def y_pieces_before(j):
    return sum(a < PIECES[j][1] for a, b in Y_PIECES)


def ssd_hi(K, e, M, j):
    a, b = PIECES[j]
    e.wait_ge(M.ynorm, y_pieces_before(j))
    for k in range(4):
        K.nc.scalar.activation(K.nh[:, k, a:b], K.z[:, k, a:b], ACT.Copy,
                               scale=K.vec[:, V_SN + k:V_SN + k + 1]).then_inc(M.mhi, 1)


def ssd_lo(K, e, M, j):
    a, b = PIECES[j]
    for k in range(4):
        e.wait_ge(M.mhi, 4 * j + k + 1)
        K.nc.vector.scalar_tensor_tensor(out=K.nl[:, k, a:b], in0=K.z[:, k, a:b],
                                         scalar=K.vec[:, V_SN + k:V_SN + k + 1],
                                         in1=K.nh[:, k, a:b].bitcast(F32), op0=ALU.mult,
                                         op1=ALU.subtract).then_inc(M.mlo, 1)


def ssd_prep_dve(K, e, M):
    V = K.nc.vector
    g = slice(SMALL_DT, SMALL_DT + SSD_H)
    e.wait_ge(M.ealog, 1)
    M.dve(V.tensor_scalar(K.go[g, 0], K.small[g, :], K.eal[g, 0:1], -1.0, ALU.mult, ALU.mult))
    M.dve(V.memset(K.go[g, 1], 1.0))
    M.dve(V.memset(K.adt, 0.0))
    M.dve(V.memset(K.go[g, 1, 0:T:P], 0.0))
    V.tensor_tensor_scan(K.adt[g, :], K.go[g, 1], K.go[g, 0], 0.0, ALU.mult, ALU.add).then_inc(M.acum, 1)


def ssd_dve(K, e, M):
    nc = K.nc
    V = nc.vector
    e.wait_ge(M.xc, 16)
    e.wait_ge(M.proj_mm, IN_START[IN_STEPS])
    V.memset(K.H[:], 0.0).then_inc(M.H, 1)
    pa = K.psf[:, :1024].rearrange("p (h q) -> p h q", h=SSD_H)
    heads = lambda t, r: t[:r].rearrange("p (h q) -> p h q", h=SSD_H)
    hv = K.H[:].rearrange("p (h q) -> p h q", h=SSD_H)

    def decays(j):
        a, r = TILES[j]
        e.wait_ge(M.a_mm, j + 1)
        e.wait_ge(M.b_mm, j + 1)
        V.tensor_copy(K.tk[:r, :], K.ps[:r, 3, 256:272]).then_inc(M.sm_read, 1)
        e.wait_ge(M.sm_read, j + 1)
        V.tensor_tensor(K.de[:r, 0:8], pa[:r, :, r - 1], K.tk[:r, 0:8], ALU.subtract).then_inc(M.de0, 1)
        for h in range(SSD_H):
            ins = V.scalar_tensor_tensor(out=K.seg[:r, j % 2, h, :r], in0=pa[:r, h, :r], scalar=K.tk[:r, h:h + 1],
                                         in1=K.msl[:r, :r], op0=ALU.subtract, op1=ALU.add)
        ins.then_inc(M.seg, 1)

    def state(j):
        a, r = TILES[j]
        e.wait_ge(M.h_read, j + 1)
        dst = K.Hp if j == TP // P - 1 else K.H
        V.tensor_tensor(K.ht[:].rearrange("p (h q) -> p h q", h=SSD_H), hv,
                        K.ea[:, j % 2, :, r - 1:r].to_broadcast([P, SSD_H, SSD_P]), ALU.mult).then_inc(M.hupd, 1)
        e.wait_ge(M.hupd, j + 1)
        e.wait_ge(M.hst_mm, j + 1)
        V.tensor_tensor(dst[:], K.ht[:], K.ps[:, 6], ALU.add).then_inc(M.hst_read, 1)
        if j == TP // P - 1:
            e.wait_ge(M.cache, 16 * (5 + GLA_H))
            V.tensor_copy(K.H[:], K.Hin).then_inc(M.H, 1)
        e.wait_ge(M.y_mm, j + 1)
        wait(e, M.y2, j)
        for u in range(4):
            ins = V.scalar_tensor_tensor(out=K.yt[:, u, :r], in0=K.xc[:, u, a:a + r],
                                         scalar=K.vec[:, V_D + u:V_D + u + 1], in1=K.ps[:, 5, P * u:P * u + r],
                                         op0=ALU.mult, op1=ALU.add)
        ins.then_inc(M.y1, 1)

    def operands(j):
        a, r = TILES[j]
        e.wait_ge(M.x_mm, j + 1)
        wait(e, M.hst_read, j)
        px = K.ps[:r, 2].rearrange("p (h q) -> p h q", h=SSD_H)
        V.tensor_tensor(heads(K.xdt, r), px, K.tk[:r, 8:16].rearrange("p (h o) -> p h o", o=1)
                        .to_broadcast([r, SSD_H, SSD_P]), ALU.mult).then_inc(M.xdt, 1)
        e.wait_ge(M.de1, j + 1)
        M.dve(V.tensor_tensor(K.de[:r, 8:16], K.de[:r, 0:8], K.tk[:r, 8:16], ALU.mult))
        V.tensor_tensor(heads(K.xde, r), px, K.de[:r, 8:16].rearrange("p (h o) -> p h o", o=1)
                        .to_broadcast([r, SSD_H, SSD_P]), ALU.mult).then_inc(M.x_read, 1)
        e.wait_ge(M.eseg, j + 1)
        e.wait_ge(M.cb2_mm, j + 1)
        for u in range(2):
            ins = V.tensor_tensor(K.seg[:r, j % 2, 4 * u:4 * u + 4, :r], K.seg[:r, j % 2, 4 * u:4 * u + 4, :r],
                                  K.ps[:r, 4, P * u:P * u + r].rearrange("p (o q) -> p o q", o=1)
                                  .to_broadcast([r, 4, r]), ALU.mult)
        ins.then_inc(M.m, 1)

    for j in range(NTT):
        decays(j)
        if j:
            state(j - 1)
        operands(j)
    state(NTT - 1)


def ssd_pool(K, e, M, outs):
    G = K.nc.gpsimd

    def carried(j):
        a, r = TILES[j]
        e.wait_ge(M.ea, j + 1)
        wait(e, M.h_read, j - 1)
        for u in range(2):
            ins = G.tensor_tensor(K.cea[:, j % 2, 4 * u:4 * u + 4, :r],
                                  K.xc[:, 6 + u, a:a + r].rearrange("p (o q) -> p o q", o=1)
                                  .to_broadcast([P, 4, r]), K.ea[:, j % 2, 4 * u:4 * u + 4, :r], ALU.mult)
        ins.then_inc(M.cea, 1)

    def norm(c):
        a, b = Y_PIECES[c]
        e.wait_ge(M.yrs, c + 1)
        z = K.z[:, :, a:b].rearrange("p (g u) q -> p g u q", g=2)
        G.tensor_tensor(z, z, K.yrms[:, :, :b - a].rearrange("p g (o q) -> p g o q", o=1)
                        .to_broadcast([P, 2, 2, b - a]), ALU.mult).then_inc(M.ynorm, 1)

    carried(0)
    for j, (a, r) in enumerate(TILES):
        if j + 1 < NTT:
            carried(j + 1)
        e.wait_ge(M.y1, j + 1)
        G.tensor_tensor(K.z[:, :, a:a + r], K.z[:, :, a:a + r], K.yt[:, :, :r], ALU.mult).then_inc(M.y2, 1)
        if y_after(j, 3) is not None:
            norm(y_after(j, 3))
        if j >= 2 and j - 2 < len(MIX_EARLY):
            k = MIX_EARLY[j - 2]
            e.wait_ge(M.mhi_early, j - 1)
            G.tensor_tensor(K.nl[:, k], mixed_tile(K, k), K.nh[:, k].bitcast(F32), ALU.subtract)\
                .then_inc(M.mlo_early, 1)
    e.dma_start(outs["ssd"][0], K.Hp[:]).then_inc(M.h_out, 16)
    norm(NYP - 2)
    norm(NYP - 1)
    e.wait_ge(M.hst_read, NTT)
    e.dma_start(outs["ssd"][1], K.H[:]).then_inc(M.h_out, 16)


def mixed_tile(K, k):
    return K.z[:, k] if k < 4 else K.gg[:, k - 4] if k < 6 else K.fq[:, k - 6]


MIX_EARLY = (6, 7, 4, 5)


def out_order(t):
    return [(m, j) for j in range(NPC) for m in range(2)] if t == 0 else [(m, j) for m in range(2) for j in range(NPC)]


def out_act(K, e, M, follow):
    nc = K.nc
    for t in range(OUT_STEPS):
        S = BASE_OUT + t
        if t:
            e.wait_ge(M.out_mm, 2 * NPC * t)
        split_hi(K, e, S + 1, (S + 1) % 2)
        if t == 0:
            e.wait_ge(M.out, 16 * MIX_OUTS)
            e.wait_ge(M.h_out, 32)
            e.wait_ge(M.out_mm, 1)
        follow_act(K, e, follow, M.out_read, 0, (2 * t, 2 * t + 1), tile_waits=t == 0)


def out_dve(K, e, M):
    V = K.nc.vector
    e.wait_ge(M.hst_read, NTT)
    e.wait_ge(M.y2, NTT)
    for j in range(NPC):
        ssd_lo(K, e, M, j)
    for t in range(OUT_STEPS):
        S = BASE_OUT + t
        split_lo(K, e, S + 1, (S + 1) % 2)
        e.wait_ge(M.x_back[t], 16)
        for n, (m, j) in enumerate(out_order(t), 2 * NPC * t):
            a, b = PIECES[j]
            d = 2 * t + m
            e.wait_ge(M.out_mm, n + 1)
            V.tensor_tensor(K.x[:, d, a:b], K.ps[:, n % 4, :b - a], K.x[:, d, a:b], ALU.add)\
                .then_inc(M.out_read, 1)


def out_pe(K, e, M):
    e.wait_ge(M.mlo_early, len(MIX_EARLY))
    for t in range(OUT_STEPS):
        S = BASE_OUT + t
        e.wait_ge(K.w_lo, 2 * (S + 1))
        whi = K.whi[:, S % 2].rearrange("p (m k n) -> p m k n", m=2, k=KT)
        wlo = K.wlo[:, S % 2].rearrange("p (m k n) -> p m k n", m=2, k=KT)
        for n, (m, j) in enumerate(out_order(t), 2 * NPC * t):
            a, b = PIECES[j]
            wait(e, M.out_read, n - 3)
            for q, k in enumerate(MIX_EARLY + (0, 1, 2, 3)):
                if t == 0 and k < 4:
                    e.wait_ge(M.mlo, 4 * j + k + 1)
                mm = three(K, K.ps[:, n % 4, :b - a], whi[:, m, k], wlo[:, m, k],
                           K.nh[:, k, a:b], K.nl[:, k, a:b], q == 0, q == KT - 1)
            mm.then_inc(M.out_mm, 1)


class NormSems:

    def __init__(self, sem, tag):
        self.sq = sem(tag + "sq")
        self.added = sem(tag + "added")
        self.sum_mm = sem(tag + "sum_mm")
        self.rstd = sem(tag + "rstd")
        self.n32 = sem(tag + "n32")
        self.hi = sem(tag + "hi")
        self.lo = sem(tag + "lo")
        self.lo_odd = sem(tag + "lo_odd")


class FfnSems:

    def __init__(self, sem, tag):
        self.sq = sem(tag + "sq")
        self.sum_mm = sem(tag + "sum_mm")
        self.rstd = sem(tag + "rstd")
        self.n32 = sem(tag + "n32")
        self.hi = sem(tag + "hi")
        self.lo = sem(tag + "lo")
        self.lo_odd = sem(tag + "lo_odd")
        self.gate_mm = sem(tag + "gate_mm")
        self.up_mm = sem(tag + "up_mm")
        self.down_mm = sem(tag + "down_mm")
        self.silu = sem(tag + "silu")
        self.h32 = sem(tag + "h32")
        self.hhi = sem(tag + "hhi")
        self.hlo = sem(tag + "hlo")
        self.x_upd = sem(tag + "x_upd")


class SoftplusSems:

    def __init__(self, sem, tag):
        self.absv = sem(tag + "absv")
        self.e = sem(tag + "e")
        self.u = sem(tag + "u")
        self.ln = sem(tag + "ln")


class MixSems:

    def __init__(self, sem, tag):
        self.proj_mm = sem(tag + "proj_mm")
        self.proj_read = sem(tag + "proj_read")
        self.chain = sem(tag + "chain")
        self.x_out = sem(tag + "x_out")
        self.cache = sem(tag + "cache")
        self.out = sem(tag + "out")
        self.kout = sem(tag + "kout")
        self.h_out = sem(tag + "h_out")
        self.fsq = sem(tag + "fsq")
        self.fss = sem(tag + "fss")
        self.fln = sem(tag + "fln")
        self.frs = sem(tag + "frs")
        self.fqk = sem(tag + "fqk")
        self.logf = sem(tag + "logf")
        self.cum = sem(tag + "cum")
        self.cb_mm = sem(tag + "cb_mm")
        self.cb = sem(tag + "cb")
        self.qz = sem(tag + "qz")
        self.s_mm = sem(tag + "s_mm")
        self.smin = sem(tag + "smin")
        self.p_exp = sem(tag + "p_exp")
        self.rinv = sem(tag + "rinv")
        self.p_scaled = sem(tag + "p_scaled")
        self.pt_mm = sem(tag + "pt_mm")
        self.pt_a = sem(tag + "pt_a")
        self.pt_v = sem(tag + "pt_v")
        self.o_mm = sem(tag + "o_mm")
        self.fo = sem(tag + "fo")
        self.g_mm = sem(tag + "g_mm")
        self.bcum = sem(tag + "bcum")
        self.eb = sem(tag + "eb")
        self.enb = sem(tag + "enb")
        self.bdiff = sem(tag + "bdiff")
        self.ebd = sem(tag + "ebd")
        self.kend = sem(tag + "kend")
        self.gqk = sem(tag + "gqk")
        self.kt_mm = sem(tag + "kt_mm")
        self.kt_read = sem(tag + "kt_read")
        self.gqm = sem(tag + "gqm")
        self.att_mm = sem(tag + "att_mm")
        self.att = sem(tag + "att")
        self.S = sem(tag + "S")
        self.st_mm = sem(tag + "st_mm")
        self.st_read = sem(tag + "st_read")
        self.S_end = sem(tag + "S_end")
        self.go_mm = sem(tag + "go_mm")
        self.go_read = sem(tag + "go_read")
        self.gsq = sem(tag + "gsq")
        self.gss = sem(tag + "gss")
        self.gln = sem(tag + "gln")
        self.grs = sem(tag + "grs")
        self.gnorm = sem(tag + "gnorm")
        self.gout = sem(tag + "gout")
        self.pad = sem(tag + "pad")
        self.prev = sem(tag + "prev")
        self.raw_tail = sem(tag + "raw_tail")
        self.tail = sem(tag + "tail")
        self.conv = sem(tag + "conv")
        self.xc = sem(tag + "xc")
        self.ealog = sem(tag + "ealog")
        self.acum = sem(tag + "acum")
        self.H = sem(tag + "H")
        self.a_mm = sem(tag + "a_mm")
        self.x_mm = sem(tag + "x_mm")
        self.b_mm = sem(tag + "b_mm")
        self.cb2_mm = sem(tag + "cb2_mm")
        self.h_read = sem(tag + "h_read")
        self.y_mm = sem(tag + "y_mm")
        self.hst_mm = sem(tag + "hst_mm")
        self.seg = sem(tag + "seg")
        self.ea = sem(tag + "ea")
        self.de0 = sem(tag + "de0")
        self.de1 = sem(tag + "de1")
        self.sm_read = sem(tag + "sm_read")
        self.cea = sem(tag + "cea")
        self.xdt = sem(tag + "xdt")
        self.x_read = sem(tag + "x_read")
        self.b_read = sem(tag + "b_read")
        self.eseg = sem(tag + "eseg")
        self.m = sem(tag + "m")
        self.hupd = sem(tag + "hupd")
        self.hst_read = sem(tag + "hst_read")
        self.y1 = sem(tag + "y1")
        self.y2 = sem(tag + "y2")
        self.ysq = sem(tag + "ysq")
        self.yss = sem(tag + "yss")
        self.yln = sem(tag + "yln")
        self.yrs = sem(tag + "yrs")
        self.ynorm = sem(tag + "ynorm")
        self.mhi_early = sem(tag + "mhi_early")
        self.mlo_early = sem(tag + "mlo_early")
        self.mhi = sem(tag + "mhi")
        self.mlo = sem(tag + "mlo")
        self.out_mm = sem(tag + "out_mm")
        self.out_read = sem(tag + "out_read")


class Core:
    pass


MIX_OUTS = 2 + 1 + 2 * GLA_H + 1


def second(u):
    return sum(len(fox_groups(j)) > 1 for _, j in FOX_UNITS[:u])


def hybrid_layer(nc, i, o):
    with ExitStack() as ctx:
        K = Core()
        K.nc, K.second = nc, second

        def sb(name, shape, dt=F32, scope=ctx):
            return scope.enter_context(nc.sbuf_tensor("sb_" + name, shape, dt))

        def sem(name):
            return ctx.enter_context(nc.semaphore(name))

        ps = ctx.enter_context(nc.psum_tensor("ps", [P, 8, 512], F32))
        K.ps = ps
        K.psf = ps[:].rearrange("p b n -> p (b n)")

        with ExitStack() as r:
            K.cea = sb("cea", [P, 2, SSD_H, P], scope=r)
            K.ea = sb("ea", [P, 2, SSD_H, P], scope=r)
            K.btok = sb("btok", [P, 256], scope=r)
        K.nh = sb("nh", [P, KT, T], F32R)
        K.wraw = sb("wraw", [P, STEP])
        K.whi = sb("whi", [P, 2, STEP], F32R)
        K.wlo = sb("wlo", [P, 2, STEP], F32R)
        K.const = sb("const", [P, NCONST])
        K.vec = sb("vec", [P, NVEC])
        K.eps = sb("eps", [P, 1])
        K.eal = sb("eal", [P, 1])
        K.cum = sb("cum", [P, CUM])
        K.adt = K.cum[:, :T]
        scratch = sb("scratch", [P, 5 * W])
        K.sq = scratch[:, :2 * W].rearrange("p (s n) -> p s n", s=2)
        K.n32 = scratch[:, 2 * W:4 * W].rearrange("p (s n) -> p s n", s=2)
        K.lnv = scratch[:, 4 * W:]
        K.qz = scratch[:, :2 * P].rearrange("p (s n) -> p s n", s=2)
        K.ysq = scratch[:, :1024].rearrange("p (t n) -> p t n", t=4)
        K.yrms = scratch[:, 1024:1536].rearrange("p (g n) -> p g n", g=2)
        c = K.const
        K.ident, K.ones, K.b64 = c[:, C_ID:C_ID + P], c[:, C_ONE:C_ONE + P], c[:, C_B64:C_B64 + P]
        K.mqk, K.msl = c[:, C_MQK:C_MQK + P], c[:, C_MSL:C_MSL + P]
        K.gmask = c[:, C_GM:C_GM + P].bitcast(I32)
        K.bmask = c[:, C_BM:C_BM + 256]

        with ExitStack() as r:
            K.seg = sb("seg", [P, 2, SSD_H, P], scope=r)
            K.xdt = sb("xdt", [P, 512], scope=r)
            K.xde = sb("xde", [P, 512], scope=r)
            K.ht = sb("ht", [P, 512], scope=r)
            K.yt = sb("yt", [P, 4, P], scope=r)
            K.tk = sb("tk", [P, 16], scope=r)
            K.de = sb("de", [P, 16], scope=r)
        K.nl = sb("nl", [P, KT, T], F32R)

        with ExitStack() as r:
            K.cb = sb("cb", [P, 2, CUM], scope=r)
            pr = sb("pr", [P, PR - 1, 1024], scope=r)
            K.pr = [pr[:, s] for s in range(PR - 1)] + [scratch[:, 2 * P:2 * P + 1024]]
            K.kc = sb("kc", [P, 2, PAST], scope=r)
            K.vc = sb("vc", [P, PAST // P, 256], scope=r)
            flat = pr[:].rearrange("p s n -> p (s n)")
            K.t1, K.t2, K.lfc = flat[:, 0:T], flat[:, T:2 * T], flat[:, 3 * 1024 - PAST:]
        with ExitStack() as r:
            K.gd = sb("gd", [P, T], scope=r)
            K.ga = sb("ga", [P, T], scope=r)
            K.gb = sb("gb", [P, T], scope=r)
            K.ge = sb("ge", [P, T], scope=r)
            K.go = sb("go", [P, 2, T], scope=r)
            K.kt = sb("kt", [P, NTT, P], scope=r)
            K.attn = sb("attn", [P, 2, GLA_H, P], scope=r)
            K.gst, K.Sin = K.gd[:, :256], K.gb[:, :256]
            K.gqm = K.ga[:, :8 * P].rearrange("p (s h q) -> p s h q", s=2, h=GLA_H)
        with ExitStack() as r:
            K.xc = sb("xc", [P, 8, T], scope=r)
        K.x = sb("x", [P, KT, T])

        with ExitStack() as r:
            sb("norm_hh0", [P, 2, T], scope=r)
            K.rms = sb("rms", [P, T], scope=r)
            sb("norm_gap", [P, 2, T], scope=r)
            K.sq_first = sb("sq_first", [P, 4, W], scope=r)
        with ExitStack() as r:
            sb("norm_low", [P, 8 * T - 4 * W], scope=r)
            K.nrm = sb("nrm", [P, 4, W], scope=r)
            K.sqs = sb("sqs", [P, 4, W], scope=r)
        with ExitStack() as r:
            K.hh = sb("hh", [P, 2, 2, T], F32R, scope=r)
            K.hl = sb("hl", [P, 2, 2, T], F32R, scope=r)
            K.sg = sb("sg", [P, 2, W], scope=r)
            K.h32 = sb("h32", [P, 2, W], scope=r)
        K.fq = sb("fq", [P, 2, T])
        K.small = sb("small", [P, T])
        with ExitStack() as r:
            K.pt = sb("pt", [P, 2, 8, P], scope=r)
        K.gg = sb("gg", [P, 2, T])
        with ExitStack() as r:
            K.gk = sb("gk", [P, T], scope=r)
            K.fk = sb("fk", [P, 2, T], scope=r)
            K.fv = sb("fv", [P, NTT, 256], scope=r)
            K.mn = sb("mn", [P, PR], scope=r)
            K.rs = sb("rs", [P, PR], scope=r)
            K.ri = sb("ri", [P, PR], scope=r)
        with ExitStack() as r:
            sb("gk_again", [P, T], scope=r)
            K.gq = sb("gq", [P, T], scope=r)
            K.gv = sb("gv", [P, NTT, 256], scope=r)
            K.S = sb("S", [P, 4, 256], scope=r)
            K.Sp = sb("S_prompt", [P, 256], scope=r)
            K.Ss = K.S[:, GCH % 4]
            K.glast = sb("glast", [P, GCH], scope=r)
        with ExitStack() as r:
            K.raw = sb("raw", [P, 2, T + 6], scope=r)
            K.acc = sb("acc", [P, 2, T + 3], scope=r)
            K.cprev = sb("cprev", [P, 8, 3], scope=r)
            K.ctail = sb("ctail", [P, 8, 2, 3], scope=r)
        with ExitStack() as r:
            K.z = sb("z", [P, 4, T], scope=r)
            sb("beside_conv", [P, 96], scope=r)
            K.H = sb("H", [P, 512], scope=r)
            K.Hp = sb("Hp", [P, 512], scope=r)
        K.Hin = K.const[:, C_MQK:C_MQK + 512]

        K.w_loaded, K.w_hi, K.w_lo = sem("w_loaded"), sem("w_hi"), sem("w_lo")
        K.x_in = [sem(f"x_in{c}") for c in range(NPC)]
        K.ones_in, K.consts_in, K.epsw, y_out = sem("ones_in"), sem("consts_in"), sem("eps_set"), sem("y_out")
        F1, F2 = FfnSems(sem, "ffn1_"), FfnSems(sem, "ffn2_")
        F2.added = sem("ffn2_added")
        M = MixSems(sem, "mix_")
        M.norm = NormSems(sem, "mixnorm_")
        M.sp, M.gsp = SoftplusSems(sem, "small_"), SoftplusSems(sem, "gla_")
        M.x_back = [sem(f"x_back{t}") for t in range(OUT_STEPS)]

        act_chain = sem("act_chain")

        block = ctx.enter_context(nc.Block())

        @block.sync
        def _(sp):
            x = i["x"].rearrange("(k p) t -> p k t", p=P)
            sp.dma_start(K.x[:, :, :W], x[:, :, :W]).then_inc(K.x_in[0], 16)
            sp.dma_start(K.ones, i["const"][:, C_ONE:C_ONE + P]).then_inc(K.ones_in, 16)
            sp.dma_start(K.vec[:], i["vec"]).then_inc(K.ones_in, 16)
            sp.dma_start(K.wraw[:], i["weights"][0]).then_inc(K.w_loaded, 16)
            for c, (a, b) in list(enumerate(PIECES))[1:]:
                sp.dma_start(K.x[:, :, a:b], x[:, :, a:b]).then_inc(K.x_in[c], 16)
            for cols in (slice(0, C_ONE), slice(C_ONE + P, NCONST)):
                sp.dma_start(K.const[:, cols], i["const"][:, cols]).then_inc(K.consts_in, 16)
            with sp.Fori(1, NSTEPS) as s:
                sp.wait_ge(K.w_lo, s * 2)
                sp.dma_start(K.wraw[:], i["weights"][s]).then_inc(K.w_loaded, 16)
            for d in range(KT):
                sp.wait_ge(F2.x_upd, DN * 10 + NPC * (d + 1))
                sp.dma_start(o["y"][d * P:(d + 1) * P], K.x[:, d]).then_inc(y_out, 16)
            sp.wait_ge(y_out, 16 * KT)

        @block.tensor
        def _(e):
            e.wait_ge(K.ones_in, 32)
            first_sum_pe(K, e, F1, 0)
            first_sum_pe(K, e, F1, 1)
            ffn_pe(K, e, F1, BASE1, first=True)
            follow_pe(K, e, M.norm)
            e.wait_ge(K.consts_in, 32)
            for t in range(IN_STEPS):
                if t == FOX_AT:
                    fox_pe(K, e, M)
                if t == GLA_GATE_AT:
                    gla_gate_pe(K, e, M)
                if t == GLA_AT:
                    gla_pe(K, e, M)
                proj_pe(K, e, M, t)
            ssd_pe(K, e, M)
            out_pe(K, e, M)
            follow_pe(K, e, F2)
            ffn_pe(K, e, F2, BASE2)

        @block.scalar
        def _(e):
            K.act = Chain(e, act_chain)
            e.wait_ge(K.epsw, 1)

            def first_split(e, N):
                if N is F2:
                    e.wait_ge(M.out_mm, NPC * KT)
            K.before_split_act = first_split

            def first_split_proj(e, M):
                e.wait_ge(F1.down_mm, DN * 11)
            K.before_split_proj = first_split_proj

            nc.scalar.preload_act_table_set(LOG_EXP)
            norm_act(K, e, F1, SUMS_FIRST)
            ffn_act(K, e, F1, BASE1, follow=M.norm)
            norm_act(K, e, M.norm, SUMS_LATER)
            e.wait_ge(K.consts_in, 32)
            for t in range(IN_STEPS):
                if t == FOX_AT:
                    fox_act(K, e, M)
                if t == GLA_AT:
                    gla_act(K, e, M)
                parts = {FOX_SMALL_AT: fox_small_act, FOX_NORM_AT: fox_norm_act, GLA_GATE_AT: gla_gate_act}
                proj_act(K, e, M, t, parts[t](K, e, M) if t in parts else {})
            ssd_act(K, e, M)
            out_act(K, e, M, follow=F2)
            norm_act(K, e, F2, SUMS_LATER)
            ffn_act(K, e, F2, BASE2)

        @block.vector
        def _(e):
            M.dve = Chain(e, M.chain)
            nc.vector.memset(K.eps[:], EPS).then_inc(K.epsw, 1)
            split_lo(K, e, 0, 0)
            e.wait_ge(K.ones_in, 32)
            norm_dve(K, e, F1, V_N1)
            ffn_dve(K, e, F1, BASE1)
            norm_dve(K, e, M.norm, V_NM)
            e.wait_ge(K.consts_in, 32)
            for t in range(IN_STEPS):
                if t == FOX_AT:
                    fox_dve(K, e, M)
                if t == GLA_AT:
                    gla_dve(K, e, M)
                split_lo(K, e, BASE_IN + t + 1, (BASE_IN + t + 1) % 2)
                if t == FOX_SMALL_AT:
                    fox_small_dve(K, e, M)
                if t == FOX_NORM_AT:
                    fox_norm_dve(K, e, M)
                if t == GLA_GATE_AT:
                    gla_gate_dve(K, e, M)
                    ssd_prep_dve(K, e, M)
                if t >= CONV_AT and IN_PLAN[t][0][0] == "x":
                    conv_dve(K, e, M, t)
            ssd_dve(K, e, M)
            out_dve(K, e, M)
            norm_dve(K, e, F2, V_N2)
            ffn_dve(K, e, F2, BASE2)

        @block.gpsimd
        def _(e):
            norm_pool(K, e, F1)
            follow_pool(K, e, M.norm)
            norm_pool(K, e, M.norm)
            e.wait_ge(F1.x_upd, DN * 11)
            e.dma_start(o["x_kept"], K.x[:]).then_inc(M.x_out, 16)
            e.wait_ge(M.x_out, 16)
            e.wait_ge(M.norm.n32, KT * NPC)
            e.dma_start(K.kc[:], i["kc"].rearrange("(t p) s -> p t s", p=P)).then_inc(M.cache, 16)
            e.dma_start(K.vc[:], i["vc"].rearrange("(t p) n -> p t n", p=P)).then_inc(M.cache, 16)
            e.dma_start(K.lfc[SMALL_FF:SMALL_FF + FOX_H], i["lfc"]).then_inc(M.cache, 16)
            fox_pool(K, e, M, o)
            e.wait_ge(M.fo, NU)
            e.wait_ge(M.kout, 16)
            e.wait_ge(M.gqk, 1)
            nc.gpsimd.memset(K.Sin, 0.0).then_inc(M.pad, 1)
            e.wait_ge(M.pad, 1)
            for h in range(GLA_H):
                r = slice(GLA_K * h, GLA_K * h + GLA_K)
                e.dma_start(K.Sin[r, 64 * h:64 * h + 64], i["gla"][r]).then_inc(M.cache, 16)
            gla_pool(K, e, M, o)
            e.wait_ge(M.go_mm, NTT)
            e.dma_start(K.cprev[:], i["cprev"].rearrange("(u p) s -> p u s", p=P)).then_inc(M.cache, 16)
            e.wait_ge(M.cache, 16 * (4 + GLA_H))
            conv_pool(K, e, M, o["tail"])
            e.wait_ge(M.proj_mm, IN_START[IN_STEPS])
            e.dma_start(K.Hin, i["ssd"]).then_inc(M.cache, 16)
            ssd_pool(K, e, M, o)
            e.wait_ge(M.y2, NTT)
            for t in range(OUT_STEPS):
                e.dma_start(K.x[:, 2 * t:2 * t + 2], o["x_kept"][:, 2 * t:2 * t + 2]).then_inc(M.x_back[t], 16)
            e.wait_ge(M.out, 16 * MIX_OUTS)
            e.wait_ge(M.h_out, 32)
            follow_pool(K, e, F2)
            norm_pool(K, e, F2)


def shape_constants():
    c = np.zeros((P, NCONST), np.float32)
    r = np.arange(P)
    c[:, C_ID:C_ID + P] = np.eye(P)
    c[:, C_ONE:C_ONE + P] = 1.0
    c[:, C_B64:C_B64 + P] = r[:, None] // 64 == r[None] // 64
    c[:, C_MQK:C_MQK + P] = np.where(r[None] <= r[:, None], 0.0, -BIG)
    c[:, C_MSL:C_MSL + P] = np.where(r[:, None] <= r[None], 0.0, -BIG)
    c[:, C_GM:C_GM + P] = (r[:, None] <= r[None]) & (r[:, None] // GLA_L == r[None] // GLA_L)
    c[:, C_BM:C_BM + 256] = r[:, None] // GLA_K == np.arange(256)[None] // GLA_V
    for h in range(SSD_H):
        c[SMALL_DT + h, C_SEL + h * P:C_SEL + (h + 1) * P] = 1.0
    for h in range(FOX_H):
        c[SMALL_FF + h, C_SEL + h * P:C_SEL + (h + 1) * P] = -8.0
    return c


def kernel(**inputs):
    import concourse.bacc as bacc
    from concourse.bass_utils import run_bass_kernel_spmd

    v = {n: np.asarray(a) for n, a in inputs.items()}
    f32 = np.float32

    def column_tile(w):
        return w.reshape(KT, P, P).transpose(1, 0, 2).reshape(P, D)

    def swiglu(gate, up, down):
        steps = []
        for kind, c in (FFN_HEAD + [(k, c + (4 if k == "up" else 2) * it) for it in range(FFN_LOOPS)
                                    for k, c in FFN_BODY] + FFN_TAIL):
            if kind == "up":
                cols = slice(P * c, P * c + P)
                steps.append(np.concatenate([column_tile(gate[:, cols]), column_tile(up[:, cols])], 1))
            else:
                steps.append(down[2 * P * c:2 * P * (c + 1)].reshape(2, P, D).transpose(1, 0, 2).reshape(P, STEP))
        return steps

    sizes = dict(z=512, x=1024, dt=8, gq=128, gk=128, gv=256, gg=256, gr=16, fq=256, fk=256, fv=256, ff=4)
    w_in, off, cols = v["w_in"][0], 0, {}
    for n, s in sizes.items():
        cols[n] = w_in[:, off:off + s]
        off += s
    small = np.zeros((D, P), f32)
    small[:, 0:GLA_R] = cols["gr"]
    small[:, SMALL_DT:SMALL_DT + SSD_H] = cols["dt"]
    small[:, SMALL_FF:SMALL_FF + FOX_H] = cols["ff"]

    def in_tile(name):
        if name in ("small", "gq", "gk"):
            return column_tile(small if name == "small" else cols[name])
        u = int(name[-1])
        return column_tile(cols[name.rstrip("0123456789")][:, P * u:P * u + P])

    steps = swiglu(v["w1_gate"][0], v["w1_up"][0], v["w1_down"][0])
    for s in IN_PLAN:
        if isinstance(s, str):
            steps.append(cols[s].reshape(KT, P, 256).transpose(1, 0, 2).reshape(P, STEP))
        else:
            tiles = [in_tile(n) for n in s] + [np.zeros((P, D), f32)] * (2 - len(s))
            steps.append(np.concatenate(tiles, 1))
    w_out = v["w_out"][0]
    for t in range(OUT_STEPS):
        steps.append(np.concatenate([column_tile(w_out[:, P * d:P * d + P]) for d in (2 * t, 2 * t + 1)], 1))
    steps += swiglu(v["w2_gate"][0], v["w2_up"][0], v["w2_down"][0])

    tiled = lambda a: a.reshape(-1, P).T
    vec = np.zeros((P, NVEC), f32)
    vec[:, V_N1:V_N1 + 8] = tiled(v["norm_ffn1"][0])
    vec[:, V_NM:V_NM + 8] = tiled(v["norm_mix"][0])
    vec[:, V_N2:V_N2 + 8] = tiled(v["norm_ffn2"][0])
    vec[:, V_CW:V_CW + 32] = v["ssd_conv_w"][0].reshape(4, 8, P).transpose(2, 1, 0).reshape(P, 32)
    vec[:, V_CB:V_CB + 8] = tiled(v["ssd_conv_b"][0])
    vec[SMALL_DT:SMALL_DT + SSD_H, V_SB] = v["ssd_dt_bias"][0]
    vec[SMALL_FF:SMALL_FF + FOX_H, V_SB] = v["fox_f_bias"][0]
    vec[SMALL_DT:SMALL_DT + SSD_H, V_AL] = v["ssd_a_log"][0]
    vec[:, V_D:V_D + 4] = tiled(np.repeat(v["ssd_d"][0], SSD_P))
    vec[:, V_SN:V_SN + 4] = tiled(v["ssd_norm"][0])
    vec[:, V_GB] = v["gla_b_gate"][0]
    vec[:, V_GN] = np.tile(v["gla_norm"][0], 2)
    vec[:, V_QN] = np.tile(v["fox_q_norm"][0], 2)
    vec[:, V_KN] = np.tile(v["fox_k_norm"][0], 2)
    const = shape_constants()
    const[:GLA_R, C_SEL:C_SEL + P] = v["gla_w_gate"][0]

    arrays = dict(
        x=np.concatenate([v["x_prompt"][0], v["x_sample"][0]], 0).T,
        weights=np.stack(steps),
        const=const, vec=vec,
        kc=v["cache_fox_k"][0, 0].reshape(PAST, 256).T,
        vc=v["cache_fox_v"][0, 0].reshape(PAST, 256),
        lfc=v["cache_fox_logf"][0, 0].T,
        gla=v["state_gla"][0, 0].reshape(P, GLA_V),
        cprev=v["state_ssd_conv"][0, 0].T,
        ssd=v["state_ssd"][0, 0].transpose(2, 0, 1).reshape(SSD_N, 512),
    )
    arrays = {n: np.ascontiguousarray(a, f32) for n, a in arrays.items()}
    out_shapes = dict(y=(D, T), tail=(P, 8, 2, 3), ssd=(2, P, 512), gla=(2, P, GLA_V), k=(P, 2, T),
                      v=(T, 256), logf=(FOX_H, T))

    nc = bacc.Bacc("TRN2", target_bir_lowering=False, num_devices=1)
    ins = {n: nc.dram_tensor(n, a.shape, F32, kind="ExternalInput").ap() for n, a in arrays.items()}
    outs = {n: nc.dram_tensor("out_" + n, s, F32, kind="ExternalOutput").ap() for n, s in out_shapes.items()}
    outs["x_kept"] = nc.dram_tensor("x_kept", (P, KT, T), F32, kind="Internal").ap()
    outs["v"] = [outs["v"][:TP].rearrange("(j p) n -> p j n", p=P),
                 outs["v"][TP:].rearrange("(j p) n -> p j n", p=TS)]
    hybrid_layer(nc, ins, outs)
    got = run_bass_kernel_spmd(nc, [arrays], core_ids=[0]).results[0]
    g = {n: got["out_" + n] for n in out_shapes}

    def rows(a, b):
        k = g["k"].transpose(2, 1, 0).reshape(T, FOX_H, FOX_D)[a:b]
        return (g["y"].T[a:b][None], k[None, None], g["v"].reshape(T, FOX_H, FOX_D)[a:b][None, None],
                g["logf"].T[a:b][None, None])

    def states(j):
        conv = g["tail"][:, :, j].transpose(2, 1, 0).reshape(1, 1, 3, 1024)
        ssd = g["ssd"][j].reshape(SSD_N, SSD_H, SSD_P).transpose(1, 2, 0)[None, None]
        return conv, ssd, g["gla"][j].reshape(1, 1, GLA_H, GLA_K, GLA_V)

    (yp, kp, vp, fp), (ys, ks, vs, fs) = rows(0, TP), rows(TP, T)
    return (yp, ys, *states(0), kp, vp, fp, *states(1), ks, vs, fs)
```
